# Optimizing a Trainium2 kernel written in Bass

```python
import jax, jax.numpy as jnp
from jax import lax
import numpy as np
import math

D_MODEL = 1024
BATCH = 1
SEQ = 256
DEPTH = 1

D_MIX = D_MODEL
CONV_CH = D_MIX // 2
CONV_WIDTH = 31
FOX_HEADS = 8
FOX_HEAD_DIM = 64
FOX_WIDTH = FOX_HEADS * FOX_HEAD_DIM
Q_BLOCK = 128
N_MEM = 256
MEM_HEADS = 4
MEM_HEAD_DIM = 128
MEM_INNER = MEM_HEADS * MEM_HEAD_DIM
D_FF = 4 * D_MODEL
EPS = 1e-6
NEG_INF = -1e30
IN_COLS = 2 * CONV_CH + 3 * FOX_WIDTH + FOX_HEADS


def rms_norm(x, g):
    xf = x.astype(jnp.float32)
    y = xf * lax.rsqrt(jnp.mean(xf * xf, axis=-1, keepdims=True) + EPS)
    return (y * g.astype(jnp.float32)).astype(x.dtype)

def layer_norm(x, g, b):
    xf = x.astype(jnp.float32)
    mu = jnp.mean(xf, axis=-1, keepdims=True)
    xc = xf - mu
    y = xc * lax.rsqrt(jnp.mean(xc * xc, axis=-1, keepdims=True) + EPS)
    return (y * g.astype(jnp.float32) + b.astype(jnp.float32)).astype(x.dtype)

def causal_depthwise_conv(u, w, b):
    out = lax.conv_general_dilated(
        u, w[:, None, :], window_strides=(1,), padding=[(CONV_WIDTH - 1, 0)],
        dimension_numbers=("NWC", "WIO", "NWC"), feature_group_count=u.shape[-1])
    return out + b

def forgetting_attention(q, k, v, log_f):
    S = q.shape[1]
    dh = q.shape[-1]
    scale = dh ** -0.5
    cum = jnp.cumsum(log_f, axis=1).transpose(0, 2, 1)
    outs = []
    for i in range(S // Q_BLOCK):
        q0 = i * Q_BLOCK
        kl = q0 + Q_BLOCK
        qb = q[:, q0:kl]
        kb = k[:, :kl]
        vb = v[:, :kl]
        logits = jnp.einsum("bqhd,bkhd->bhqk", qb, kb,
                            preferred_element_type=jnp.float32) * scale
        logits = logits + cum[:, :, q0:kl, None] - cum[:, :, None, :kl]
        q_pos = q0 + jnp.arange(Q_BLOCK)
        k_pos = jnp.arange(kl)
        mask = k_pos[None, :] <= q_pos[:, None]
        p = jax.nn.softmax(jnp.where(mask, logits, NEG_INF), axis=-1)
        outs.append(jnp.einsum("bhqk,bkhd->bqhd", p.astype(vb.dtype), vb))
    return jnp.concatenate(outs, axis=1)

def hybrid_mixer(h, w_in, b_forget, conv_w, conv_b, conv_ln_g, conv_ln_b, w_out):
    B, S, _ = h.shape
    z = h @ w_in
    o = 0
    a = z[..., o:o + CONV_CH]; o += CONV_CH
    g = z[..., o:o + CONV_CH]; o += CONV_CH
    q = z[..., o:o + FOX_WIDTH]; o += FOX_WIDTH
    k = z[..., o:o + FOX_WIDTH]; o += FOX_WIDTH
    v = z[..., o:o + FOX_WIDTH]; o += FOX_WIDTH
    f_logit = z[..., o:o + FOX_HEADS]

    u = a * jax.nn.sigmoid(g)
    u = causal_depthwise_conv(u, conv_w, conv_b)
    u = jax.nn.silu(layer_norm(u, conv_ln_g, conv_ln_b))

    log_f = jax.nn.log_sigmoid((f_logit + b_forget).astype(jnp.float32))
    shp = (B, S, FOX_HEADS, FOX_HEAD_DIM)
    att = forgetting_attention(q.reshape(shp), k.reshape(shp), v.reshape(shp), log_f)
    att = att.reshape(B, S, FOX_WIDTH)

    return jnp.concatenate([u, att], axis=-1) @ w_out

def memory_cross_attention(h, mem_n, w_mq, w_mk, w_mv, w_mo):
    B, S, _ = h.shape
    q = (h @ w_mq).reshape(B, S, MEM_HEADS, MEM_HEAD_DIM)
    k = (mem_n @ w_mk).reshape(B, N_MEM, MEM_HEADS, MEM_HEAD_DIM)
    v = (mem_n @ w_mv).reshape(B, N_MEM, MEM_HEADS, MEM_HEAD_DIM)
    logits = jnp.einsum("bqhd,bmhd->bhqm", q, k,
                        preferred_element_type=jnp.float32) * (MEM_HEAD_DIM ** -0.5)
    p = jax.nn.softmax(logits, axis=-1)
    out = jnp.einsum("bhqm,bmhd->bqhd", p.astype(v.dtype), v).reshape(B, S, MEM_INNER)
    return out @ w_mo

def squared_relu_mlp(h, w_up, w_down):
    return jnp.square(jax.nn.relu(h @ w_up)) @ w_down

def first_inputs(seed: int = 0) -> dict:
    key = jax.random.key(seed)
    ks = jax.random.split(key, 24)
    nrm = lambda k, shape, fan_in: jax.random.normal(k, shape, jnp.float32) * (fan_in ** -0.5)
    gain = lambda k, shape: 1.0 + 0.05 * jax.random.normal(k, shape, jnp.float32)
    small = lambda k, shape: 0.02 * jax.random.normal(k, shape, jnp.float32)
    L = DEPTH
    return {
        "x": jax.random.normal(ks[0], (BATCH, SEQ, D_MODEL), jnp.float32),
        "mem": jax.random.normal(ks[1], (BATCH, N_MEM, D_MODEL), jnp.float32),
        "norm_mix_pre": gain(ks[2], (L, D_MODEL)),
        "norm_mix_post": gain(ks[3], (L, D_MODEL)),
        "w_in": nrm(ks[4], (L, D_MODEL, IN_COLS), D_MODEL),
        "b_forget": jax.random.uniform(ks[5], (L, FOX_HEADS), jnp.float32, 1.0, 5.0),
        "conv_w": nrm(ks[6], (L, CONV_WIDTH, CONV_CH), CONV_WIDTH),
        "conv_b": small(ks[7], (L, CONV_CH)),
        "conv_ln_g": gain(ks[8], (L, CONV_CH)),
        "conv_ln_b": small(ks[9], (L, CONV_CH)),
        "w_out": nrm(ks[10], (L, D_MIX, D_MODEL), D_MIX),
        "norm_mem_pre": gain(ks[11], (L, D_MODEL)),
        "norm_mem_post": gain(ks[12], (L, D_MODEL)),
        "norm_memkv": gain(ks[13], (L, D_MODEL)),
        "w_mq": nrm(ks[14], (L, D_MODEL, MEM_INNER), D_MODEL),
        "w_mk": nrm(ks[15], (L, D_MODEL, MEM_INNER), D_MODEL),
        "w_mv": nrm(ks[16], (L, D_MODEL, MEM_INNER), D_MODEL),
        "w_mo": nrm(ks[17], (L, MEM_INNER, D_MODEL), MEM_INNER),
        "norm_mlp_pre": gain(ks[18], (L, D_MODEL)),
        "norm_mlp_post": gain(ks[19], (L, D_MODEL)),
        "w_up": nrm(ks[20], (L, D_MODEL, D_FF), D_MODEL),
        "w_down": nrm(ks[21], (L, D_FF, D_MODEL), D_FF),
    }

def first_block(x, mem, norm_mix_pre, norm_mix_post, w_in, b_forget, conv_w, conv_b,
              conv_ln_g, conv_ln_b, w_out, norm_mem_pre, norm_mem_post, norm_memkv,
              w_mq, w_mk, w_mv, w_mo, norm_mlp_pre, norm_mlp_post, w_up, w_down):
    for l in range(DEPTH):
        h = rms_norm(x, norm_mix_pre[l])
        y = hybrid_mixer(h, w_in[l], b_forget[l], conv_w[l], conv_b[l],
                         conv_ln_g[l], conv_ln_b[l], w_out[l])
        x = x + rms_norm(y, norm_mix_post[l])
        h = rms_norm(x, norm_mem_pre[l])
        mem_n = rms_norm(mem, norm_memkv[l])
        y = memory_cross_attention(h, mem_n, w_mq[l], w_mk[l], w_mv[l], w_mo[l])
        x = x + rms_norm(y, norm_mem_post[l])
        h = rms_norm(x, norm_mlp_pre[l])
        y = squared_relu_mlp(h, w_up[l], w_down[l])
        x = x + rms_norm(y, norm_mlp_post[l])
    return x


N_META = 16
D_MIX_2 = 2 * D_MODEL
SSD_HEAD_DIM = 64
SSD_HEADS = 24
D_SSD = SSD_HEADS * SSD_HEAD_DIM
SSD_GROUPS = 4
SSD_STATE = 128
SSD_CONV = 4
SSD_CHUNK = 128
D_XBC = D_SSD + 2 * SSD_GROUPS * SSD_STATE
D_SC = D_MIX_2 - D_SSD
SC_CONV = 3
D_IN = D_SSD + D_XBC + SSD_HEADS + 3 * D_SC
PEER_HEADS = 8
PEER_KEYS = 128
PEER_EXPERTS = PEER_KEYS * PEER_KEYS
PEER_TOPK = 16
PEER_QDIM = 256
PEER_HALF = PEER_QDIM // 2
PEER_BLOCK = 512


def rmsnorm(x, g):
    xf = x.astype(jnp.float32)
    xf = xf * lax.rsqrt(jnp.mean(xf * xf, axis=-1, keepdims=True) + EPS)
    return (xf * g.astype(jnp.float32)).astype(x.dtype)

def causal_dwconv(x, w):
    width, ch = w.shape
    return lax.conv_general_dilated(
        x, w[:, None, :].astype(x.dtype), window_strides=(1,), padding=[(width - 1, 0)],
        dimension_numbers=('NWC', 'WIO', 'NWC'), feature_group_count=ch)

def segsum(a):
    t = a.shape[-1]
    ar = jnp.broadcast_to(a[..., None], a.shape + (t,))
    ar = jnp.where(jnp.tril(jnp.ones((t, t), bool), -1), ar, 0.0)
    cs = jnp.cumsum(ar, axis=-2)
    return jnp.where(jnp.tril(jnp.ones((t, t), bool), 0), cs, -jnp.inf)

def ssd_scan(x, dt, A, Bm, Cm):
    b, l, h, p = x.shape
    g, n = Bm.shape[2], Bm.shape[3]
    r, q = h // g, SSD_CHUNK
    c = l // q
    xc = x.reshape(b, c, q, g, r, p)
    Bc = Bm.reshape(b, c, q, g, n)
    Cc = Cm.reshape(b, c, q, g, n)
    dtc = dt.reshape(b, c, q, g, r)
    a = (dtc * A.reshape(g, r)).transpose(0, 3, 4, 1, 2)
    x_dt = xc * dtc[..., None]
    a_cs = jnp.cumsum(a, axis=-1)
    decay_in = jnp.exp(segsum(a))
    cb = jnp.einsum('bclgn,bcsgn->bgcls', Cc, Bc)
    y_diag = jnp.einsum('bgcls,bgrcls,bcsgrp->bclgrp', cb, decay_in, x_dt)
    decay_states = jnp.exp(a_cs[..., -1:] - a_cs)
    states = jnp.einsum('bcsgn,bgrcs,bcsgrp->bcgrpn', Bc, decay_states, x_dt)
    states = jnp.concatenate([jnp.zeros_like(states[:, :1]), states], axis=1)
    chunk_a = jnp.pad(a_cs[..., -1], ((0, 0), (0, 0), (0, 0), (1, 0)))
    decay_chunk = jnp.exp(segsum(chunk_a))
    new_states = jnp.einsum('bgrzc,bcgrpn->bzgrpn', decay_chunk, states)
    prev_states = new_states[:, :-1]
    y_off = jnp.einsum('bclgn,bcgrpn,bgrcl->bclgrp', Cc, prev_states, jnp.exp(a_cs))
    return (y_diag + y_off).reshape(b, l, h, p)

def hybrid_mixer_2(n, w_in, conv_ssd_w, conv_ssd_b, dt_bias, a_log, d_skip, ssd_norm_w,
                 conv_sc_w, w_out):
    bsz, L, _ = n.shape
    proj = n @ w_in.astype(n.dtype)
    s1 = D_SSD
    s2 = s1 + D_XBC
    s3 = s2 + SSD_HEADS
    s4 = s3 + D_SC
    s5 = s4 + D_SC
    z, xbc, dt_raw, sc_b, sc_c, sc_x = jnp.split(proj, [s1, s2, s3, s4, s5], axis=-1)

    xbc = jax.nn.silu(causal_dwconv(xbc, conv_ssd_w) + conv_ssd_b.astype(n.dtype))
    xs, Bm, Cm = jnp.split(xbc, [D_SSD, D_SSD + SSD_GROUPS * SSD_STATE], axis=-1)
    xs_h = xs.reshape(bsz, L, SSD_HEADS, SSD_HEAD_DIM)
    dt = jax.nn.softplus(dt_raw.astype(jnp.float32) + dt_bias.astype(jnp.float32))
    A = -jnp.exp(a_log.astype(jnp.float32))
    pad_len = SSD_CHUNK - N_META

    def lpad(t):
        return jnp.pad(t, ((0, 0), (pad_len, 0)) + ((0, 0),) * (t.ndim - 2))

    y = ssd_scan(lpad(xs_h.astype(jnp.float32)), lpad(dt), A,
                 lpad(Bm.reshape(bsz, L, SSD_GROUPS, SSD_STATE).astype(jnp.float32)),
                 lpad(Cm.reshape(bsz, L, SSD_GROUPS, SSD_STATE).astype(jnp.float32)))
    y = y[:, pad_len:] + d_skip.astype(jnp.float32)[:, None] * xs_h.astype(jnp.float32)
    y = y.reshape(bsz, L, D_SSD) * jax.nn.silu(z.astype(jnp.float32))
    y_ssd = rmsnorm(y.reshape(bsz, L, SSD_GROUPS, D_SSD // SSD_GROUPS),
                    ssd_norm_w.reshape(SSD_GROUPS, D_SSD // SSD_GROUPS))
    y_ssd = y_ssd.reshape(bsz, L, D_SSD).astype(n.dtype)

    y_sc = sc_b * causal_dwconv(sc_c * sc_x, conv_sc_w)

    return jnp.concatenate([y_ssd, y_sc], axis=-1) @ w_out.astype(n.dtype)

def peer_ffn(n, w_q, sub_keys, expert_u, expert_v):
    bsz, L, d = n.shape
    t = n.reshape(-1, d)
    T = t.shape[0]
    q = (t @ w_q.astype(n.dtype)).reshape(T, PEER_HEADS, 2, PEER_HALF)
    s = jnp.einsum('thsd,hskd->thsk', q, sub_keys.astype(n.dtype)).astype(jnp.float32)
    v_half, i_half = lax.top_k(s, PEER_TOPK)
    cand = (v_half[:, :, 0, :, None] + v_half[:, :, 1, None, :]).reshape(T, PEER_HEADS, PEER_TOPK * PEER_TOPK)
    best, pos = lax.top_k(cand, PEER_TOPK)
    i1 = jnp.take_along_axis(i_half[:, :, 0], pos // PEER_TOPK, axis=-1)
    i2 = jnp.take_along_axis(i_half[:, :, 1], pos % PEER_TOPK, axis=-1)
    experts = (i1 * PEER_KEYS + i2).reshape(T, PEER_HEADS * PEER_TOPK)
    gates = jax.nn.softmax(best, axis=-1).reshape(T, PEER_HEADS * PEER_TOPK).astype(n.dtype)

    nb = -(-T // PEER_BLOCK)
    padT = nb * PEER_BLOCK - T
    tp = jnp.pad(t, ((0, padT), (0, 0))).reshape(nb, PEER_BLOCK, d)
    ep = jnp.pad(experts, ((0, padT), (0, 0))).reshape(nb, PEER_BLOCK, -1)
    gp = jnp.pad(gates, ((0, padT), (0, 0))).reshape(nb, PEER_BLOCK, -1)

    def block(args):
        xb, eb, gb = args
        u = expert_u[eb].astype(xb.dtype)
        act = jax.nn.gelu(jnp.einsum('td,tkd->tk', xb, u), approximate=False) * gb
        return jnp.einsum('tk,tkd->td', act, expert_v[eb].astype(xb.dtype))

    out = lax.map(block, (tp, ep, gp))
    return out.reshape(-1, d)[:T].reshape(bsz, L, d)

def second_inputs(seed: int = 0) -> dict:
    key = jax.random.key(seed)
    ks = jax.random.split(key, 20)

    def nrm(k, shape, scale):
        return jax.random.normal(k, shape, jnp.float32) * scale

    x = nrm(ks[0], (BATCH, SEQ, D_MODEL), 1.0)
    meta_tokens = nrm(ks[1], (N_META, D_MODEL), 1.0)
    g_mix = 1.0 + nrm(ks[2], (DEPTH, D_MODEL), 0.05)
    w_in = nrm(ks[3], (DEPTH, D_MODEL, D_IN), D_MODEL ** -0.5)
    conv_ssd_w = nrm(ks[4], (DEPTH, SSD_CONV, D_XBC), SSD_CONV ** -0.5)
    conv_ssd_b = nrm(ks[5], (DEPTH, D_XBC), 0.02)
    dt0 = jnp.exp(jax.random.uniform(ks[6], (DEPTH, SSD_HEADS), jnp.float32,
                                     minval=math.log(1e-3), maxval=math.log(1e-1)))
    dt_bias = dt0 + jnp.log(-jnp.expm1(-dt0))
    a_log = jnp.log(jax.random.uniform(ks[7], (DEPTH, SSD_HEADS), jnp.float32, minval=1.0, maxval=16.0))
    d_skip = 1.0 + nrm(ks[8], (DEPTH, SSD_HEADS), 0.05)
    ssd_norm_w = 1.0 + nrm(ks[9], (DEPTH, D_SSD), 0.05)
    conv_sc_w = nrm(ks[10], (DEPTH, SC_CONV, D_SC), SC_CONV ** -0.5)
    w_out = nrm(ks[11], (DEPTH, D_MIX_2, D_MODEL), D_MIX_2 ** -0.5)
    g_ffn = 1.0 + nrm(ks[12], (DEPTH, D_MODEL), 0.05)
    w_q = nrm(ks[13], (DEPTH, D_MODEL, PEER_HEADS * PEER_QDIM), D_MODEL ** -0.5)
    sub_keys = nrm(ks[14], (DEPTH, PEER_HEADS, 2, PEER_KEYS, PEER_HALF), PEER_HALF ** -0.5)
    expert_u = nrm(ks[15], (DEPTH, PEER_EXPERTS, D_MODEL), D_MODEL ** -0.5)
    expert_v = nrm(ks[16], (DEPTH, PEER_EXPERTS, D_MODEL), PEER_HEADS ** -0.5)
    g_final = 1.0 + nrm(ks[17], (D_MODEL,), 0.05)
    return {"x": x, "meta_tokens": meta_tokens, "g_mix": g_mix, "w_in": w_in,
            "conv_ssd_w": conv_ssd_w, "conv_ssd_b": conv_ssd_b, "dt_bias": dt_bias,
            "a_log": a_log, "d_skip": d_skip, "ssd_norm_w": ssd_norm_w,
            "conv_sc_w": conv_sc_w, "w_out": w_out, "g_ffn": g_ffn, "w_q": w_q,
            "sub_keys": sub_keys, "expert_u": expert_u, "expert_v": expert_v,
            "g_final": g_final}

def second_block(x, meta_tokens, g_mix, w_in, conv_ssd_w, conv_ssd_b, dt_bias, a_log, d_skip,
              ssd_norm_w, conv_sc_w, w_out, g_ffn, w_q, sub_keys, expert_u, expert_v, g_final):
    bsz = x.shape[0]
    meta = jnp.broadcast_to(meta_tokens[None].astype(x.dtype), (bsz, N_META, D_MODEL))
    h = jnp.concatenate([meta, x], axis=1)
    for l in range(DEPTH):
        h = h + hybrid_mixer_2(rmsnorm(h, g_mix[l]), w_in[l], conv_ssd_w[l], conv_ssd_b[l],
                             dt_bias[l], a_log[l], d_skip[l], ssd_norm_w[l], conv_sc_w[l], w_out[l])
        h = h + peer_ffn(rmsnorm(h, g_ffn[l]), w_q[l], sub_keys[l], expert_u[l], expert_v[l])
    h = rmsnorm(h, g_final)
    return h[:, N_META:]


def setup_inputs(seed=0):
    out = dict(first_inputs(seed))
    for name, value in second_inputs(seed + 1).items():
        if name != "x":
            out[name + "_2"] = value
    return out


def reference(
    x, mem, norm_mix_pre, norm_mix_post, w_in, b_forget, conv_w, conv_b, conv_ln_g, conv_ln_b,
    w_out, norm_mem_pre, norm_mem_post, norm_memkv, w_mq, w_mk, w_mv, w_mo, norm_mlp_pre,
    norm_mlp_post, w_up, w_down, meta_tokens_2, g_mix_2, w_in_2, conv_ssd_w_2, conv_ssd_b_2,
    dt_bias_2, a_log_2, d_skip_2, ssd_norm_w_2, conv_sc_w_2, w_out_2, g_ffn_2, w_q_2,
    sub_keys_2, expert_u_2, expert_v_2, g_final_2,
):
    x = first_block(
        x, mem, norm_mix_pre, norm_mix_post, w_in, b_forget, conv_w, conv_b, conv_ln_g,
        conv_ln_b, w_out, norm_mem_pre, norm_mem_post, norm_memkv, w_mq, w_mk, w_mv, w_mo,
        norm_mlp_pre, norm_mlp_post, w_up, w_down,
    )
    return second_block(
        x, meta_tokens_2, g_mix_2, w_in_2, conv_ssd_w_2, conv_ssd_b_2, dt_bias_2, a_log_2,
        d_skip_2, ssd_norm_w_2, conv_sc_w_2, w_out_2, g_ffn_2, w_q_2, sub_keys_2, expert_u_2,
        expert_v_2, g_final_2,
    )


_drawn_inputs = setup_inputs


def setup_inputs(seed=0):
    import zlib

    import numpy as np

    out = dict(_drawn_inputs(seed))
    spreads = {}
    factors = {'conv_ln_b': 3.039, 'conv_ssd_b_2': 4.47, 'd_skip_2': 4.028, 'g_ffn_2': 3.04}
    for name, (base, spread) in spreads.items():
        noise = np.random.default_rng([zlib.crc32(name.encode()), seed]).standard_normal(out[name].shape)
        drawn = base * np.exp(spread * noise) if base else spread * noise
        out[name] = __import__('jax').numpy.asarray(drawn.astype(out[name].dtype))
    for name, factor in factors.items():
        out[name] = (out[name] * factor).astype(out[name].dtype)
    return out
```

```python
from contextlib import ExitStack

import numpy as np

import concourse.bass as bass
from concourse import mybir

P = 128
F32 = mybir.dt.float32
F32R = mybir.dt.float32r
U32 = mybir.dt.uint32
ACT = mybir.ActivationFunctionType
ALU = mybir.AluOpType
AX_X = mybir.AxisListType.X

D = 1024
KT = D // P
T = 256
TT = T // P
EPS = 1e-6
NEG = -1e30
SLOTS = 4
BLK = 1024

CONV_CH, CONV_W = 512, 31
CT = CONV_CH // P
FOX_H, FOX_D = 8, 64
MEM_H, MEM_D = 4, 128
FF_CHUNKS = 4 * D // P
META = 16
SSD_H, SSD_D, SSD_G = 24, 64, 4
HG = SSD_H // SSD_G
GW = HG * SSD_D
D_SSD = SSD_H * SSD_D
XBC_T = (D_SSD + 2 * SSD_G * P) // P
XS_T = D_SSD // P
SC_T = 4
TM = META + T
PEER_H, TOPK, KEYS = 8, 16, 128
HK = PEER_H * TOPK

STREAM = {}
N_BLOCKS = 0
for _name, _n in (("ag", 8), ("qk", 8), ("v", 4), ("mk", 4), ("mv", 4), ("wout", 8), ("mq", 4), ("mo", 4),
                  ("mlp", 2 * FF_CHUNKS), ("xbc", XBC_T), ("sc", 3 * SC_T), ("z", 12), ("wout2", 16),
                  ("wq", 16), ("peer", 2 * KEYS)):
    STREAM[_name] = N_BLOCKS
    N_BLOCKS += _n

GAINS = 6
COL = {}
N_COLS = 0
for _name, _n in (("conv_w", CT * CONV_W), ("conv_b", CT), ("ln_g", CT), ("ln_b", CT), ("ssd_w", XBC_T * 4),
                  ("ssd_b", XBC_T), ("sc_w", SC_T * 3), ("w_f", KT * FOX_H), ("w_dt", KT * SSD_H)):
    COL[_name] = N_COLS
    N_COLS += _n
ROW = {}
N_ROWS = 0
for _name, _n in (("b_forget", FOX_H), ("dt_bias", SSD_H), ("a_log", SSD_H), ("d_skip", SSD_H),
                  ("ssd_norm", D_SSD)):
    ROW[_name] = N_ROWS
    N_ROWS += _n


class Steps:

    def __init__(self, eng, sem):
        self.eng, self.sem, self.n = eng, sem, 0

    def __call__(self, ins):
        ins.then_inc(self.sem, 1)
        self.n += 1
        return self.n

    def wait(self, n=None):
        self.eng.wait_ge(self.sem, self.n if n is None else n)


def build(nc, stream, gain_cols, cols, rows, post_gains, x, mem, meta, keys_in, out, h2_spill):
    ctx = ExitStack()
    with ctx:
        def sb(name, shape, dt=F32):
            return ctx.enter_context(nc.sbuf_tensor(name, shape, dt))

        def ps(name, shape):
            return ctx.enter_context(nc.psum_tensor(name, shape, F32))

        def sem(name):
            return ctx.enter_context(nc.semaphore(name))

        raw = sb("raw", [P, SLOTS, BLK])
        wh = sb("wh", [P, SLOTS, BLK], F32R)
        wl = sb("wl", [P, SLOTS, BLK], F32R)
        x_at = (nc.sbuf_base + 31) // 32 * 32
        X = sb("X", [P, TT, D])
        xh_at = (nc.sbuf_base + 31) // 32 * 32
        xh = sb("xh", [P, KT, TM], F32R)
        xl = sb("xl", [P, KT, TM], F32R)
        ident = sb("ident", [P, P])
        upper = sb("upper", [P, P])
        neg_half = sb("neg_half", [P, 1])
        later = sb("later", [P, P])
        ones = sb("ones", [P, P])
        iota = sb("iota", [P, P])
        gain = sb("gain", [P, GAINS * KT])
        stat = sb("stat", [P, 48])
        i1T = sb("i1T", [P, T])
        i2T = sb("i2T", [P, T])
        gT = sb("gT", [P, T])
        arena_at = (nc.sbuf_base + 31) // 32 * 32
        gates = sb("gates", [P, KEYS, T])

        def at(name, shape, offset, dt=F32, base=None):
            return nc.alloc_sbuf_tensor_at(name, shape, dt, offset=(arena_at if base is None else base) + offset)

        colp = at("colp", [P, N_COLS], 0)
        rowp = at("rowp", [P, N_ROWS], 2304)
        rowg = at("rowg", [P, 3, D], 8768)
        mask = at("mask", [P, 2 * P], 21056)
        memx = at("memx", [P, TT, D], 22080)
        AG = at("AG", [P, 2 * CT, T], 30272)
        QK = at("QK", [P, 8, T], 38464)
        V = at("V", [P, TT, 512], 46656)
        UP = at("UP", [P, CT, CONV_W - 1 + T], 50752)
        CV = at("CV", [P, CT, T], 55328)
        SQ = at("SQ", [P, CT, T], 59424)
        xn = at("xn", [P, 3, D], 63520)
        mh = at("mh", [P, KT, T], 79904, F32R)
        ml = at("ml", [P, KT, T], 88096, F32R)
        MK = at("MK", [P, 4, T], 96288)
        MV = at("MV", [P, TT, 512], 100384)
        DEC = at("DEC", [P, FOX_H, 3, P], 104480)
        att_s = at("att_s", [P, 2, 2 * P], 116768)
        att_p = at("att_p", [P, 2, 2 * P], 118816)
        att_pt = at("att_pt", [P, 2, 2, P], 120864)
        mixh = at("mixh", [P, 8, T], 22080, F32R)
        mixl = at("mixl", [P, 8, T], 30272, F32R)
        moh = at("moh", [P, 4, T], 38464, F32R)
        mol = at("mol", [P, 4, T], 42560, F32R)
        MQ = at("MQ", [P, 4, T], 46656)
        mlp_hid = at("mlp_hid", [P, 2, T], 50752)
        mlp_act = at("mlp_act", [P, 2, T], 52800)
        mlp_ah = at("mlp_ah", [P, 2, T], 54848, F32R)
        mlp_al = at("mlp_al", [P, 2, T], 56896, F32R)
        metax = at("metax", [META, D], 124192)
        SCX = at("SCX", [P, 3 * SC_T, TM], 8768)
        SP = at("SP", [P, SC_T, 2 + TM], 21824)
        sct = at("sct", [P, 2, T], 26240)
        SP_tmp = at("SP_tmp", [P, T], 124192)
        Z = at("Z", [P, TT, D_SSD], 28288)
        m2h = at("m2h", [P, 16, T], 40576, F32R)
        m2l = at("m2l", [P, 16, T], 56960, F32R)
        XB = at("XB", [P, XBC_T, 3 + TM], 79904)
        XS = at("XS", [P, XBC_T, TM], 102432)
        XT = at("XT", [P, 3, D_SSD], 79904)
        BN = at("BN", [P, 2, 4 * P], 98336)
        XDT = at("XDT", [P, TT, D_SSD], 8768)
        XDD = at("XDD", [P, D_SSD], 21056)
        ST = at("ST", [P, D_SSD], 0, base=xh_at)
        YO = at("YO", [P, D_SSD], 6144, base=xh_at)
        CBM = at("CBM", [P, 4, P], 12288, base=xh_at)
        AU = at("AU", [P, 2, 3, P], 124192)
        EE = at("EE", [P, 2, 3, P], 127264)
        MM = at("MM", [P, 2, 3, P], 73344)
        dtz = at("dtz", [P, 4, 72], 76416)
        exs = at("exs", [P, 120], 77568)
        QP = at("QP", [P, 16, T], 8768)
        cand = at("cand", [P, PEER_H, TOPK * TOPK], 33344)
        cand2 = at("cand2", [P, PEER_H, TOPK * TOPK], 41536)
        eqs = at("eqs", [P, HK, TOPK], 49728)
        keys = at("keys", [P, 16, KEYS], 79904)
        SCO = at("SCO", [P, TT, 16, KEYS], 88096)
        SCO2 = at("SCO2", [P, 16, KEYS], 104480)
        V16 = at("V16", [P, 16, TOPK], 112672)
        I16 = at("I16", [P, 16, TOPK], 113696, U32)
        I16F = at("I16F", [P, 16, TOPK], 114720)
        BV = at("BV", [P, PEER_H, TOPK], 115744)
        PU = at("PU", [P, PEER_H, TOPK], 116256, U32)
        PA = at("PA", [P, 2, HK], 116768, U32)
        PF = at("PF", [P, 2, HK], 117792)
        NAT = at("NAT", [P, 3, HK], 118816)
        gsum = at("gsum", [P, 2 * PEER_H], 120352)
        hotA = at("hotA", [P, 2, 4, KEYS], 0, base=x_at)
        hotB = at("hotB", [P, 2, 4, KEYS], 4096, base=x_at)
        peer_hid = at("peer_hid", [P, 2, T], 0, base=x_at)
        peer_act = at("peer_act", [P, 2, T], 2048, base=x_at)
        peer_ah = at("peer_ah", [P, 2, T], 4096, F32R, base=x_at)
        peer_al = at("peer_al", [P, 2, T], 6144, F32R, base=x_at)
        fin_x = at("fin_x", [P, TT, D], 0)
        fin_g = at("fin_g", [P, D], 8192)
        fin_t = at("fin_t", [P, TT, D], 12288)
        fin_j = at("fin_j", [P, TT, D], 20480)

        Y = ps("Y", [P, TT, D])
        AO = ps("AO", [P, 2, 512])
        M = ps("M", [P, 2, 512])

        landed = [sem(f"landed{s}") for s in range(SLOTS)]
        split_hi, split_lo = sem("split_hi"), sem("split_lo")
        w_used = sem("w_used")
        a_free = sem("a_free")
        x_in, mem_in, par_in, row_in = sem("x_in"), sem("mem_in"), sem("par_in"), sem("row_in")
        meta_in, keys_land = sem("meta_in"), sem("keys_land")
        consts = sem("consts")
        vec_step, act_step, pool_step = sem("vec_step"), sem("act_step"), sem("pool_step")
        norm_ss, norm_rstd, norm_scaled = sem("norm_ss"), sem("norm_rstd"), sem("norm_scaled")
        norm_turned, norm_hi, norm_lo = sem("norm_turned"), sem("norm_hi"), sem("norm_lo")
        v_out, f_prod, mv_out = sem("v_out"), sem("f_prod"), sem("mv_out")
        gate_sig, conv_pad = sem("gate_sig"), sem("conv_pad")
        conv_step, conv_done = sem("conv_step"), sem("conv_done")
        f_z, f_ln, logf, dec_done = sem("f_z"), sem("f_ln"), sem("logf"), sem("dec_done")
        ln_sum, ln_xc, ln_sq, ln_y, ln_silu, ln_hi, ln_lo = (sem(n) for n in (
            "ln_sum", "ln_xc", "ln_sq", "ln_y", "ln_silu", "ln_hi", "ln_lo"))
        at_logit, at_max, at_neg, at_exp, at_inv, at_p = (sem(n) for n in (
            "at_logit", "at_max", "at_neg", "at_exp", "at_inv", "at_p"))
        at_turn, at_pt, at_pv, at_hi, at_lo = (sem(n) for n in ("at_turn", "at_pt", "at_pv", "at_hi", "at_lo"))
        post_ss, post_rstd, post_y, x_ready = sem("post_ss"), sem("post_rstd"), sem("post_y"), sem("x_ready")
        hid_prod, hid_hi, hid_lo, hid_out = sem("hid_prod"), sem("hid_hi"), sem("hid_lo"), sem("hid_out")
        xconv, xsilu, z_out = sem("xconv"), sem("xsilu"), sem("z_out")
        dt_prod, dt_z, dt_ln, dt_a = sem("dt_prod"), sem("dt_z"), sem("dt_ln"), sem("dt_a")
        sc_y, sc_hi, sc_lo = sem("sc_y"), sem("sc_hi"), sem("sc_lo")
        tr_in, tr_out = sem("tr_in"), sem("tr_out")
        cb_prod, cb_mask, ac_prod, ac_exp = sem("cb_prod"), sem("cb_mask"), sem("ac_prod"), sem("ac_exp")
        top_sub_own = sem("top_sub_own")
        xdd_w, xdd_done, xdt_done, xd_done = sem("xdd_w"), sem("xdd_done"), sem("xdt_done"), sem("xd_done")
        st_prod, st_done = sem("st_prod"), sem("st_done")
        au_done, seg_prod, seg_exp, seg_m, y_prod = (sem(n) for n in (
            "au_done", "seg_prod", "seg_exp", "seg_m", "y_prod"))
        off_prod, off_done, y_add, y_gate = sem("off_prod"), sem("off_done"), sem("y_add"), sem("y_gate")
        grp_ss, grp_rstd, grp_y, y_turn, y_hi, y_lo = (sem(n) for n in (
            "grp_ss", "grp_rstd", "grp_y", "y_turn", "y_hi", "y_lo"))
        spilled, s_prod, s_out = sem("spilled"), sem("s_prod"), sem("s_out")
        top_sub, top_exp, top_nat, top_turn, top_T = (sem(n) for n in (
            "top_sub", "top_exp", "top_nat", "top_turn", "top_T"))
        hot_a, hot_b, g_prod, g_out = sem("hot_a"), sem("hot_b"), sem("g_prod"), sem("g_out")
        ln_var, ln_rstd, fin_rstd = sem("ln_var"), sem("ln_rstd"), sem("fin_rstd")
        fin_in, fin_ss, fin_y, stored = sem("fin_in"), sem("fin_ss"), sem("fin_y"), sem("stored")

        LAST = {k: STREAM[k] + n for k, n in (("qk", 8), ("ag", 8), ("v", 4), ("mk", 4), ("mv", 4), ("wout", 8),
                                              ("mq", 4), ("mo", 4), ("mlp", 2 * FF_CHUNKS), ("xbc", XBC_T),
                                              ("sc", 12), ("z", 12), ("wout2", 16), ("wq", 16),
                                              ("peer", 2 * KEYS))}
        A_BASE = {}
        n_a = 0
        for name, n in (("ag", 8), ("qk", 8), ("mk", 4), ("mq", 4), ("mlp", FF_CHUNKS), ("xbc", XBC_T),
                        ("sc", 12), ("wq", 16), ("peer", KEYS)):
            A_BASE[name] = n_a
            n_a += n

        def up_block(b0, c):
            return b0 if c == 0 else b0 + 2 * c - 1

        def down_block(b0, c, n):
            return b0 + 2 * c + 2 if c < n - 1 else b0 + 2 * n - 1

        def pieces(n):
            two = [(X[:, j, :], P, j * P) for j in range(TT)]
            if n == 1:
                return [(memx[:, j, :], P, j * P) for j in range(TT)], mh, ml
            if n == 0 or n in (2, 3, 5):
                return two, xh, xl
            return [(s, r, META + c) for s, r, c in two] + [(metax[:, :], META, 0)], xh, xl

        NORM_TILES = [2, 2, 2, 2, 3, 2]

        units = [("fox", h, j) for h in range(FOX_H) for j in range(TT)]
        fox_units = len(units)
        units += [("mem", h, j) for h in range(MEM_H) for j in range(TT)]

        def unit_keys(u):
            kind, _, j = units[u]
            return P * (j + 1) if kind == "fox" else T

        def unit_dest(u):
            kind, h, j = units[u]
            if kind == "fox":
                r = FOX_D * (h % 2)
                return slice(r, r + FOX_D), mixh[:, CT + h // 2, P * j:P * j + P], mixl[:, CT + h // 2, P * j:P * j + P]
            return slice(0, P), moh[:, h, P * j:P * j + P], mol[:, h, P * j:P * j + P]

        block = ctx.enter_context(nc.Block())

        @block.sync
        def _(sp):
            sp.dma_start(X[:, :, :], x).then_inc(x_in, 16)
            for s in range(SLOTS):
                sp.dma_start(raw[:, s, :], stream[s]).then_inc(landed[s], 16)
            with sp.Fori(1, N_BLOCKS // SLOTS) as i:
                for s in range(SLOTS):
                    sp.wait_ge(split_lo, i * SLOTS + s - 3)
                    sp.dma_start(raw[:, s, :], stream[i * SLOTS + s]).then_inc(landed[s], 16)

        @block.scalar
        def _(act):
            step = Steps(act, act_step)
            act.dma_start(gain[:, :], gain_cols).then_inc(par_in, 16)
            act.dma_start(colp[:, :], cols).then_inc(par_in, 16)
            act.dma_start(rowp[:, :], rows.partition_broadcast(P)).then_inc(row_in, 16)
            act.dma_start(memx[:, :, :], mem).then_inc(mem_in, 16)
            for n in range(3):
                act.dma_start(rowg[:, n, :], post_gains[n].partition_broadcast(P)).then_inc(row_in, 16)
            act.dma_start(metax[:, :], meta).then_inc(meta_in, 16)

            def split(b0, j, i=0):
                b = b0 + j
                s = b % SLOTS
                act.wait_ge(landed[s], (i + b // SLOTS + 1) * 16)
                if not (type(i) is int and 4 * i + b < 4):
                    act.wait_ge(w_used, i * 4 + (b - 3))
                nc.scalar.copy(wh[:, s, :], raw[:, s, :]).then_inc(split_hi, 1)

            def split_ahead(b0, n):
                for j in range(n):
                    split(b0 + 4, j)

            def norm(n, ready=None):
                tiles, dh, _ = pieces(n)
                t0 = sum(NORM_TILES[:n])
                for k, (src, r, c) in enumerate(tiles):
                    if ready:
                        ready(k)
                    nc.scalar.activation(xn[0:r, k, :], src, ACT.Square,
                                         accum_out=stat[0:r, k:k + 1]).then_inc(norm_ss, 1)
                for k, (src, r, c) in enumerate(tiles):
                    act.wait_ge(norm_rstd, t0 + k + 1)
                    nc.scalar.activation(xn[0:r, k, :], src, ACT.Copy, scale=stat[0:r, 8 + k:9 + k])\
                        .then_inc(norm_scaled, 1)
                for k, (src, r, c) in enumerate(tiles):
                    for q in range(2):
                        g = 2 * (t0 + k) + q
                        act.wait_ge(norm_turned, g + 1)
                        for i in range(4):
                            kt = 4 * q + i
                            ins = nc.scalar.activation(dh[:, kt, c:c + r], M[:, g % 2, P * i:P * i + r], ACT.Copy,
                                                       scale=gain[:, n * KT + kt:n * KT + kt + 1])
                        ins.then_inc(norm_hi, 1)

            def evac(name, j, dest, n=T, scale=1.0, i=0, func=ACT.Copy):
                e = A_BASE[name] + j
                act.wait_ge(w_used, i * 4 + (STREAM[name] + j + 1))
                nc.scalar.activation(dest, AO[:, e % 2, 0:n], func, scale=scale).then_inc(a_free, 1)

            for j in range(SLOTS):
                split(0, j)
            act.wait_ge(par_in, 32)
            norm(0, lambda k: act.wait_ge(x_in, 16) if k == 0 else None)
            for j in range(8):
                evac("ag", j, AG[:, j, :])
                split(STREAM["ag"] + 4, j)
            step.eng.wait_ge(a_free, 8)
            nc.scalar.activation(AG[:, CT:, :], AG[:, CT:, :], ACT.Sigmoid).then_inc(gate_sig, 1)
            for j in range(8):
                evac("qk", j, QK[:, j, :], scale=FOX_D ** -0.5 if j < 4 else 1.0)
                split(STREAM["qk"] + 4, j)
            split_ahead(STREAM["v"], 4)
            act.wait_ge(w_used, LAST["v"])
            nc.scalar.copy(V[:, :, :], Y[:, 0, :].rearrange("p (j c) -> p j c", j=TT)).then_inc(v_out, 1)
            act.wait_ge(f_z, 2)
            step(nc.scalar.activation(stat[:, 32:48], stat[:, 32:48], ACT.Exp))
            step.wait()
            nc.scalar.activation(stat[:, 32:48], stat[:, 32:48], ACT.Ln, bias=1.0).then_inc(f_ln, 1)
            norm(1, lambda k: act.wait_ge(mem_in, 16) if k == 0 else None)
            for j in range(4):
                evac("mk", j, MK[:, j, :])
                split(STREAM["mk"] + 4, j)
            split_ahead(STREAM["mv"], 4)
            act.wait_ge(w_used, LAST["mv"])
            nc.scalar.copy(MV[:, :, :], Y[:, 1, :].rearrange("p (j c) -> p j c", j=TT)).then_inc(mv_out, 1)
            act.wait_ge(ln_xc, 1)
            nc.scalar.activation(SQ[:, :, :], CV[:, :, :], ACT.Square).then_inc(ln_sq, 1)
            act.wait_ge(ln_y, 1)
            for c in range(CT):
                ins = nc.scalar.activation(SQ[:, c, :], CV[:, c, :], ACT.Silu,
                                           bias=colp[:, COL["ln_b"] + c:COL["ln_b"] + c + 1],
                                           scale=colp[:, COL["ln_g"] + c:COL["ln_g"] + c + 1])
            ins.then_inc(ln_silu, 1)
            act.wait_ge(ln_silu, 1)
            nc.scalar.copy(mixh[:, 0:CT, :], SQ[:, :, :]).then_inc(ln_hi, 1)

            def attention(first, last):
                for s in range(first, last + 3):
                    u = s
                    if u < last:
                        act.wait_ge(at_neg, u + 1)
                        if u >= 2:
                            act.wait_ge(at_turn, u - 1)
                        nk = unit_keys(u)
                        nc.scalar.activation(att_p[:, u % 2, 0:nk], att_s[:, u % 2, 0:nk], ACT.Exp,
                                             bias=stat[:, 18 + u % 2:19 + u % 2],
                                             accum_out=stat[:, 20 + u % 2:21 + u % 2]).then_inc(at_exp, 1)
                    u = s - 2
                    if first <= u < last:
                        act.wait_ge(at_turn, u + 1)
                        if u >= 2:
                            act.wait_ge(at_pv, u - 1)
                        n = unit_keys(u)
                        nc.scalar.copy(att_pt[:, u % 2, :, :].rearrange("p a b -> p (a b)")[:, 0:n],
                                       Y[:, 0, 512 * (u % 2):512 * (u % 2) + n]).then_inc(at_pt, 1)
                    u = s - 3
                    if first <= u < last:
                        rows_, dh, _ = unit_dest(u)
                        act.wait_ge(at_pv, u + 1)
                        nc.scalar.copy(dh[rows_, :], Y[rows_, 1, 512 * (u % 2):512 * (u % 2) + P])\
                            .then_inc(at_hi, 1)

            attention(0, fox_units)

            def post(p):
                for j in range(TT):
                    nc.scalar.activation(xn[:, j, :], Y[:, j, :], ACT.Square,
                                         accum_out=stat[:, 4 + j:5 + j]).then_inc(post_ss, 1)

            split_ahead(STREAM["wout"], 8)
            act.wait_ge(w_used, LAST["wout"])
            post(0)
            norm(2, lambda k: act.wait_ge(x_ready, k + 1))
            for j in range(4):
                evac("mq", j, MQ[:, j, :], scale=MEM_D ** -0.5)
                split(STREAM["mq"] + 4, j)
            attention(fox_units, len(units))
            split_ahead(STREAM["mo"], 4)
            act.wait_ge(w_used, LAST["mo"])
            post(1)
            norm(3, lambda k: act.wait_ge(x_ready, 2 + k + 1))

            def mlp(name, n, hid, act_, ah, func, base):
                b0 = STREAM[name]

                def hidden(s, i):
                    b = b0 if type(i) is int and i + s == 0 else b0 + 2 * s - 1
                    act.wait_ge(w_used, i * 4 + (b + 1))
                    nc.scalar.activation(hid[:, s, :], AO[:, s, 0:T], func).then_inc(a_free, 1)

                def high(s, i):
                    act.wait_ge(hid_prod, i * 2 + (base + s + 1))
                    nc.scalar.copy(ah[:, s, :], act_[:, s, :]).then_inc(hid_hi, 1)

                for s in range(2):
                    hidden(s, 0)
                    split(up_block(b0, s) + 4, 0)
                    high(s, 0)
                    if s:
                        split(down_block(b0, 0, n) + 4, 0)
                with act.Fori(1, n // 2 - 1) as i:
                    for s in range(2):
                        hidden(s, i)
                        split(b0 - 1 + 2 * s + 4, 0, i)
                        high(s, i)
                        split(b0 - 1 + 2 * s + 5, 0, i)
                i = n // 2 - 1
                for s in range(2):
                    c = 2 * i + s
                    hidden(s, i)
                    if up_block(b0, c) + 4 < N_BLOCKS:
                        split(up_block(b0, c) + 4, 0)
                    high(s, i)
                    if b0 + 2 * c + 4 < N_BLOCKS:
                        split(b0 + 2 * c + 4, 0)
                if b0 + 2 * n - 1 + 4 < N_BLOCKS:
                    split(b0 + 2 * n - 1 + 4, 0)

            mlp("mlp", FF_CHUNKS, mlp_hid, mlp_act, mlp_ah, ACT.Copy, 0)
            post(2)

            def ready4(k):
                if k == TT:
                    act.wait_ge(meta_in, 16)
                else:
                    act.wait_ge(x_ready, 4 + k + 1)
            norm(4, ready4)
            act.wait_ge(dt_z, 2)
            step(nc.scalar.activation(dtz[0:META, 1, 0:24], dtz[0:META, 1, 0:24], ACT.Exp))
            step(nc.scalar.activation(dtz[:, 1, 24:72], dtz[:, 1, 24:72], ACT.Exp))
            step(nc.scalar.activation(rowp[:, ROW["a_log"]:ROW["a_log"] + SSD_H],
                                      rowp[:, ROW["a_log"]:ROW["a_log"] + SSD_H], ACT.Exp))
            step.wait()
            nc.scalar.activation(dtz[0:META, 1, 0:24], dtz[0:META, 1, 0:24], ACT.Ln, bias=1.0).then_inc(dt_ln, 1)
            nc.scalar.activation(dtz[:, 1, 24:72], dtz[:, 1, 24:72], ACT.Ln, bias=1.0).then_inc(dt_ln, 1)
            for j in range(4):
                evac("xbc", j, XB[:, j, 3:], TM)
                split(STREAM["xbc"] + 4, j)
            with act.Fori(1, XBC_T // 4) as i:
                for j in range(4):
                    evac("xbc", j, XB[:, i * 4 + j, 3:], TM, i=i)
                    split(STREAM["xbc"] + 4, j, i)
                act.wait_ge(xconv, i * 16)
                nc.scalar.activation(XS[:, bass.ds(i * 4 - 4, 4), :], XS[:, bass.ds(i * 4 - 4, 4), :], ACT.Silu)\
                    .then_inc(xsilu, 1)
            act.wait_ge(xconv, 4 * XBC_T)
            nc.scalar.activation(XS[:, XBC_T - 4:, :], XS[:, XBC_T - 4:, :], ACT.Silu).then_inc(xsilu, 1)
            with act.Fori(0, SC_T * 3 // 4) as i:
                for j in range(4):
                    evac("sc", j, SCX[:, i * 4 + j, :], TM, i=i)
                    split(STREAM["sc"] + 4, j, i)
            for g in range(3):
                split_ahead(STREAM["z"] + 4 * g, 4)
                act.wait_ge(w_used, STREAM["z"] + 4 * g + 4)
                nc.scalar.activation(Z[:, :, 512 * g:512 * g + 512],
                                     Y[:, g % 2, :].rearrange("p (j c) -> p j c", j=TT), ACT.Silu).then_inc(z_out, 1)
            for k in range(SC_T):
                act.wait_ge(sc_y, k + 1)
                nc.scalar.copy(m2h[:, XS_T + k, :], sct[:, k % 2, :]).then_inc(sc_hi, 1)
            n_tr = 0
            for c in range(3):
                r = META if c == 0 else P
                for q in range(4 if c < 2 else 3):
                    act.wait_ge(tr_in, n_tr + 1)
                    dst = XT[0:r, c, 512 * q:512 * q + 512] if q < 3 else BN[0:r, c, :]
                    nc.scalar.copy(dst, M[0:r, n_tr % 2, :]).then_inc(tr_out, 1)
                    n_tr += 1
            act.wait_ge(ac_prod, 1)
            nc.scalar.activation(exs[:, 0:96], AO[:, 1, 0:96], ACT.Exp).then_inc(ac_exp, 1)
            nc.scalar.activation(exs[0:META, 96:120], AO[0:META, 1, 96:120], ACT.Exp).then_inc(ac_exp, 1)
            for c in range(TT):
                for s in range(8):
                    k = 8 * c + s
                    act.wait_ge(seg_prod, k + 1)
                    if k >= 2:
                        act.wait_ge(seg_m, k - 1)
                    nc.scalar.activation(EE[:, k % 2, :, :].rearrange("p a b -> p (a b)"), AO[:, k % 2, 0:3 * P],
                                         ACT.Exp).then_inc(seg_exp, 1)
                for g in range(SSD_G):
                    act.wait_ge(y_gate, c + 1)
                    nc.scalar.activation(XT[:, c + 1, GW * g:GW * g + GW], YO[:, GW * g:GW * g + GW], ACT.Square,
                                         accum_out=stat[:, 24 + g:25 + g]).then_inc(grp_ss, 1)
                for q in range(3):
                    act.wait_ge(y_turn, 3 * c + q + 1)
                    nc.scalar.copy(m2h[:, 4 * q:4 * q + 4, P * c:P * c + P],
                                   M[:, (3 * c + q) % 2, :].rearrange("p (k t) -> p k t", k=4)).then_inc(y_hi, 1)
            split_ahead(STREAM["wout2"], 16)
            norm(5, lambda k: act.wait_ge(x_ready, 6 + k + 1))
            with act.Fori(0, 4) as i:
                for j in range(4):
                    evac("wq", j, QP[:, i * 4 + j, :], i=i)
                    split(STREAM["wq"] + 4, j, i)
            for q in range(8):
                act.wait_ge(s_prod, q + 1)
                nc.scalar.copy(SCO[:, q // 4, 4 * (q % 4):4 * (q % 4) + 4, :].rearrange("p a b -> p (a b)"),
                               Y[:, (q // 2) % 2, 512 * (q % 2):512 * (q % 2) + 512]).then_inc(s_out, 1)
            for j in range(TT):
                act.wait_ge(top_sub, j + 1)
                nc.scalar.activation(BV[:, :, :], BV[:, :, :], ACT.Exp).then_inc(top_exp, 1)
                act.wait_ge(top_turn, j + 1)
                for n, d in enumerate((i1T, i2T, gT)):
                    ins = nc.scalar.copy(d[:, P * j:P * j + P], M[:, j, P * n:P * n + P])
                ins.then_inc(top_T, 1)
            with act.Fori(0, T // 8) as i:
                for s in range(2):
                    act.wait_ge(g_prod, i * 2 + s + 1)
                    nc.scalar.copy(gates[:, :, bass.ds(i * 8 + 4 * s, 4)],
                                   M[:, s, :].rearrange("p (t k) -> p k t", t=4)).then_inc(g_out, 1)
            mlp("peer", KEYS, peer_hid, peer_act, peer_ah, ACT.Gelu, FF_CHUNKS)
            act.wait_ge(w_used, N_BLOCKS)
            act.wait_ge(spilled, 16)
            act.wait_ge(hid_prod, FF_CHUNKS + KEYS)
            act.dma_start(fin_x[:, :, :], h2_spill).then_inc(fin_in, 16)
            act.dma_start(fin_g[:, :], post_gains[3].partition_broadcast(P)).then_inc(fin_in, 16)
            for j in range(TT):
                act.wait_ge(fin_y, j + 1)
                nc.scalar.activation(fin_j[:, j, :], fin_t[:, j, :], ACT.Square,
                                     accum_out=stat[:, 4 + j:5 + j]).then_inc(fin_ss, 1)
            for j in range(TT):
                act.wait_ge(fin_y, 2 + j + 1)
                act.dma_start(out[:, j, :], fin_x[:, j, :]).then_inc(stored, 16)
            act.wait_ge(stored, 32)

        @block.vector
        def _(dve):
            step = Steps(dve, vec_step)

            def split(b0, j, i=0):
                b = b0 + j
                dve.wait_ge(split_hi, i * 4 + (b + 1))
                s = b % SLOTS
                nc.vector.tensor_tensor(wl[:, s, :], raw[:, s, :], wh[:, s, :].bitcast(F32), ALU.subtract)\
                    .then_inc(split_lo, 1)

            def split_ahead(b0, n):
                for j in range(n):
                    split(b0 + 4, j)

            def norm(n):
                tiles, dh, dl = pieces(n)
                t0 = sum(NORM_TILES[:n])
                for k, (src, r, c) in enumerate(tiles):
                    for q in range(2):
                        g = 2 * (t0 + k) + q
                        dve.wait_ge(norm_hi, g + 1)
                        for i in range(4):
                            kt = 4 * q + i
                            ins = nc.vector.scalar_tensor_tensor(
                                out=dl[:, kt, c:c + r], in0=M[:, g % 2, P * i:P * i + r],
                                scalar=gain[:, n * KT + kt:n * KT + kt + 1],
                                in1=dh[:, kt, c:c + r].bitcast(F32), op0=ALU.mult, op1=ALU.subtract)
                        ins.then_inc(norm_lo, 1)

            def col(name, k):
                return colp[:, COL[name] + k:COL[name] + k + 1]

            nc.vector.memset(UP[:, :, 0:CONV_W - 1], 0.0).then_inc(conv_pad, 1)
            for j in range(SLOTS):
                split(0, j)
            dve.wait_ge(par_in, 32)
            norm(0)
            split_ahead(STREAM["ag"], 8)
            dve.wait_ge(gate_sig, 1)
            nc.vector.tensor_tensor(UP[:, :, CONV_W - 1:], AG[:, 0:CT, :], AG[:, CT:, :], ALU.mult)\
                .then_inc(conv_pad, 1)
            dve.wait_ge(conv_pad, 2)

            taps = [(w, c) for w in range(CONV_W) for c in range(CT)]

            def conv(k):
                w, c = taps[k]
                src = UP[:, c, w:w + T]
                if w == 0:
                    nc.vector.tensor_scalar(CV[:, c, :], src, col("conv_w", c * CONV_W), col("conv_b", c),
                                            ALU.mult, ALU.add).then_inc(conv_step, 1)
                else:
                    dve.wait_ge(conv_step, k - CT + 1)
                    nc.vector.scalar_tensor_tensor(out=CV[:, c, :], in0=src,
                                                   scalar=col("conv_w", c * CONV_W + w), in1=CV[:, c, :],
                                                   op0=ALU.mult, op1=ALU.add).then_inc(conv_step, 1)

            done = [0]

            def some_taps(n):
                for k in range(done[0], min(done[0] + n, len(taps))):
                    conv(k)
                done[0] = min(done[0] + n, len(taps))

            for j in range(8):
                split(STREAM["qk"] + 4, j)
                some_taps(6)
            for j in range(4):
                split(STREAM["v"] + 4, j)
                some_taps(6)
            dve.wait_ge(f_prod, 1)
            dve.wait_ge(row_in, 64)
            z8 = stat[:, 32:48].rearrange("p (j h) -> p j h", j=TT)
            zf = SQ[:, 0, 0:16].rearrange("p (j h) -> p j h", j=TT)
            bf = rowp[:, ROW["b_forget"]:ROW["b_forget"] + FOX_H]
            step(nc.vector.tensor_tensor(zf, M[:, 0, 0:16].rearrange("p (j h) -> p j h", j=TT),
                                         bf[:, None, :].to_broadcast([P, TT, FOX_H]), ALU.add))
            step.wait()
            nc.vector.scalar_tensor_tensor(out=z8, in0=zf, scalar=-1.0, in1=zf, op0=ALU.mult, op1=ALU.min)\
                .then_inc(f_z, 1)
            nc.vector.tensor_scalar(zf, zf, 0.0, None, ALU.min).then_inc(f_z, 1)
            some_taps(6)
            dve.wait_ge(f_ln, 1)
            nc.vector.tensor_tensor(zf, zf, z8, ALU.subtract).then_inc(logf, 1)
            norm(1)
            for j in range(4):
                split(STREAM["mk"] + 4, j)
                some_taps(8)
            for j in range(4):
                split(STREAM["mv"] + 4, j)
                some_taps(8)
            some_taps(len(taps))
            dve.wait_ge(conv_step, len(taps))
            nc.vector.tensor_copy(stat[:, 14:15], CV[:, 0, 0:1]).then_inc(conv_done, 1)
            dve.wait_ge(ln_sum, 1)
            nc.vector.scalar_tensor_tensor(out=CV[:, :, :], in0=M[:, 0, 0:T][:, None, :].to_broadcast([P, CT, T]),
                                           scalar=-1.0 / CONV_CH, in1=CV[:, :, :], op0=ALU.mult, op1=ALU.add)\
                .then_inc(ln_xc, 1)
            dve.wait_ge(ln_sum, 2)
            v = UP[:, 0, 0:T]
            nc.vector.tensor_scalar(v, M[:, 1, 0:T], 1.0 / CONV_CH, EPS, ALU.mult, ALU.add).then_inc(ln_var, 1)
            dve.wait_ge(ln_rstd, 1)
            nc.vector.tensor_tensor(CV[:, :, :], CV[:, :, :], v[:, None, :].to_broadcast([P, CT, T]), ALU.mult)\
                .then_inc(ln_y, 1)
            dve.wait_ge(ln_hi, 1)
            nc.vector.tensor_tensor(mixl[:, 0:CT, :], SQ[:, :, :], mixh[:, 0:CT, :].bitcast(F32), ALU.subtract)\
                .then_inc(ln_lo, 1)

            def attention(first, last):
                for s in range(first, last + 4):
                    u = s
                    if u < last:
                        kind, _, j = units[u]
                        nk = unit_keys(u)
                        m = mask[:, P:2 * P] if (kind, j) == ("fox", 0) else mask[:, 0:2 * P] if kind == "fox" \
                            else None
                        dve.wait_ge(at_logit, u + 1)
                        if u >= 2:
                            dve.wait_ge(at_exp, u - 1)
                        if m is None:
                            step(nc.vector.tensor_copy(att_s[:, u % 2, 0:nk], M[:, u % 2, 0:nk]))
                            nc.vector.tensor_reduce(stat[:, 16 + u % 2:17 + u % 2], M[:, u % 2, 0:nk], AX_X,
                                                    ALU.max).then_inc(at_max, 1)
                        else:
                            nc.vector.tensor_tensor_reduce(att_s[:, u % 2, 0:nk], M[:, u % 2, 0:nk], m, 1.0, 3 * NEG,
                                                           ALU.add, ALU.max, stat[:, 16 + u % 2:17 + u % 2])\
                                .then_inc(at_max, 1)
                        dve.wait_ge(at_max, u + 1)
                        nc.vector.tensor_scalar(stat[:, 18 + u % 2:19 + u % 2], stat[:, 16 + u % 2:17 + u % 2],
                                                -1.0, None, ALU.mult).then_inc(at_neg, 1)
                    u = s - 1
                    if first <= u < last:
                        dve.wait_ge(at_exp, u + 1)
                        nc.vector.reciprocal(stat[:, 22 + u % 2:23 + u % 2], stat[:, 20 + u % 2:21 + u % 2])\
                            .then_inc(at_inv, 1)
                        dve.wait_ge(at_inv, u + 1)
                        nk = unit_keys(u)
                        nc.vector.tensor_scalar(att_p[:, u % 2, 0:nk], att_p[:, u % 2, 0:nk],
                                                stat[:, 22 + u % 2:23 + u % 2], None, ALU.mult).then_inc(at_p, 1)
                    u = s - 3
                    if first <= u < last:
                        rows_, dh, dl = unit_dest(u)
                        dve.wait_ge(at_hi, u + 1)
                        nc.vector.tensor_tensor(dl[rows_, :], Y[rows_, 1, 512 * (u % 2):512 * (u % 2) + P],
                                                dh[rows_, :].bitcast(F32), ALU.subtract).then_inc(at_lo, 1)

            def post(p):
                for j in range(TT):
                    dve.wait_ge(post_rstd, 2 * p + j + 1)
                    nc.vector.scalar_tensor_tensor(out=xn[:, j, :], in0=Y[:, j, :], scalar=stat[:, 12 + j:13 + j],
                                                   in1=rowg[:, p, :], op0=ALU.mult, op1=ALU.mult)\
                        .then_inc(post_y, 1)
                    dve.wait_ge(post_y, 2 * p + j + 1)
                    nc.vector.tensor_tensor(X[:, j, :], X[:, j, :], xn[:, j, :], ALU.add).then_inc(x_ready, 1)

            attention(0, fox_units)
            split_ahead(STREAM["wout"], 8)
            post(0)
            norm(2)
            split_ahead(STREAM["mq"], 4)
            attention(fox_units, len(units))
            split_ahead(STREAM["mo"], 4)
            post(1)
            norm(3)

            def squared_relu(hid, dst, c):
                return nc.vector.scalar_tensor_tensor(out=dst, in0=hid, scalar=0.0, in1=hid,
                                                      op0=ALU.max, op1=ALU.mult)

            def weighed(hid, dst, c):
                return nc.vector.tensor_tensor(dst, hid, gates[:, c, :], ALU.mult)

            def mlp(name, n, hid, act_, ah, al, func, free_base, base):
                b0 = STREAM[name]

                def hidden(c, s, i):
                    dve.wait_ge(a_free, i * 2 + (free_base + s + 1))
                    func(hid[:, s, :], act_[:, s, :], c).then_inc(hid_prod, 1)

                def low(s, i):
                    dve.wait_ge(hid_hi, i * 2 + (base + s + 1))
                    nc.vector.tensor_tensor(al[:, s, :], act_[:, s, :], ah[:, s, :].bitcast(F32), ALU.subtract)\
                        .then_inc(hid_lo, 1)

                for s in range(2):
                    hidden(s, s, 0)
                    split(up_block(b0, s) + 4, 0)
                    low(s, 0)
                    if s:
                        split(down_block(b0, 0, n) + 4, 0)
                with dve.Fori(1, n // 2 - 1) as i:
                    for s in range(2):
                        hidden(i * 2 + s, s, i)
                        split(b0 - 1 + 2 * s + 4, 0, i)
                        low(s, i)
                        split(b0 - 1 + 2 * s + 5, 0, i)
                for s in range(2):
                    i = n // 2 - 1
                    c = 2 * i + s
                    hidden(c, s, i)
                    if up_block(b0, c) + 4 < N_BLOCKS:
                        split(up_block(b0, c) + 4, 0)
                    low(s, i)
                    if down_block(b0, c - 1, n) + 4 < N_BLOCKS:
                        split(down_block(b0, c - 1, n) + 4, 0)
                if down_block(b0, n - 1, n) + 4 < N_BLOCKS:
                    split(down_block(b0, n - 1, n) + 4, 0)

            mlp("mlp", FF_CHUNKS, mlp_hid, mlp_act, mlp_ah, mlp_al, squared_relu, A_BASE["mlp"], 0)
            post(2)

            norm(4)
            step(nc.vector.memset(XB[:, :, 0:3], 0.0))
            dve.wait_ge(dt_prod, 1)
            db = rowp[:, ROW["dt_bias"]:ROW["dt_bias"] + SSD_H]
            ea = rowp[:, ROW["a_log"]:ROW["a_log"] + SSD_H]
            parts = ((META, 0, 1), (P, 24, 2))
            for r, o, n in parts:
                step(nc.vector.tensor_tensor(dtz[0:r, 0, o:o + 24 * n].rearrange("p (j h) -> p j h", j=n),
                                             M[0:r, 0, o:o + 24 * n].rearrange("p (j h) -> p j h", j=n),
                                             db[0:r, None, :].to_broadcast([r, n, SSD_H]), ALU.add))
            step.wait()
            for r, o, n in parts:
                z = dtz[0:r, 0, o:o + 24 * n]
                nc.vector.scalar_tensor_tensor(out=dtz[0:r, 1, o:o + 24 * n], in0=z, scalar=-1.0, in1=z,
                                               op0=ALU.mult, op1=ALU.min).then_inc(dt_z, 1)
            dve.wait_ge(dt_ln, 2)
            for r, o, n in parts:
                step(nc.vector.scalar_tensor_tensor(out=dtz[0:r, 2, o:o + 24 * n], in0=dtz[0:r, 0, o:o + 24 * n],
                                                    scalar=0.0, in1=dtz[0:r, 1, o:o + 24 * n],
                                                    op0=ALU.max, op1=ALU.add))
            step.wait()
            for r, o, n in parts:
                nc.vector.scalar_tensor_tensor(
                    out=dtz[0:r, 3, o:o + 24 * n].rearrange("p (j h) -> p j h", j=n),
                    in0=dtz[0:r, 2, o:o + 24 * n].rearrange("p (j h) -> p j h", j=n), scalar=-1.0,
                    in1=ea[0:r, None, :].to_broadcast([r, n, SSD_H]), op0=ALU.mult, op1=ALU.mult)\
                    .then_inc(dt_a, 1)

            def conv4(i):
                for w in range(4):
                    for j in range(4):
                        src = XB[:, i * 4 + j, w:w + TM]
                        dst = XS[:, i * 4 + j, :]
                        o = COL["ssd_w"]
                        wt = colp[:, bass.ds(i * 16 + (o + 4 * j + w), 1)]
                        if w == 0:
                            bias = colp[:, bass.ds(i * 4 + (COL["ssd_b"] + j), 1)]
                            nc.vector.tensor_scalar(dst, src, wt, bias, ALU.mult, ALU.add).then_inc(xconv, 1)
                        else:
                            dve.wait_ge(xconv, i * 16 + (4 * w + j - 3))
                            nc.vector.scalar_tensor_tensor(out=dst, in0=src, scalar=wt, in1=dst,
                                                           op0=ALU.mult, op1=ALU.add).then_inc(xconv, 1)

            with dve.Fori(0, XBC_T // 4) as i:
                for j in range(4):
                    split(STREAM["xbc"] + 4, j, i)
                dve.wait_ge(a_free, i * 4 + (A_BASE["xbc"] + 4))
                conv4(i)
            with dve.Fori(0, SC_T * 3 // 4) as i:
                for j in range(4):
                    split(STREAM["sc"] + 4, j, i)
            for j in range(12):
                split(STREAM["z"] + 4, j)
            for k in range(SC_T):
                dve.wait_ge(sc_hi, k + 1)
                nc.vector.tensor_tensor(m2l[:, XS_T + k, :], sct[:, k % 2, :], m2h[:, XS_T + k, :].bitcast(F32),
                                        ALU.subtract).then_inc(sc_lo, 1)
            dve.wait_ge(ac_exp, 2)
            nc.vector.tensor_tensor(exs[0:META, 96:120], exs[0:META, 96:120], dtz[0:META, 2, 0:24], ALU.mult)\
                .then_inc(xdd_w, 1)
            nc.vector.tensor_tensor(exs[:, 48:72], exs[:, 48:72], dtz[:, 2, 24:48], ALU.mult).then_inc(xdd_w, 1)

            def heads(t, o=0):
                return t[:, o:o + GW].rearrange("p (h d) -> p h d", h=HG)

            def per_head(col0, g, n=HG, w=SSD_D):
                return exs[:, col0 + HG * g:col0 + HG * g + n][:, :, None].to_broadcast([P, n, w])

            for g in range(SSD_G):
                dve.wait_ge(st_prod, g + 1)
                nc.vector.tensor_copy(ST[:, GW * g:GW * g + GW], M[:, g % 2, 0:GW]).then_inc(st_done, 1)
            for c in range(TT):
                dve.wait_ge(cb_prod, c + 1)
                nc.vector.tensor_tensor(CBM[:, :, :], M[:, 0, :].rearrange("p (g l) -> p g l", g=SSD_G),
                                        upper[:, None, :].to_broadcast([P, SSD_G, P]), ALU.mult).then_inc(cb_mask, 1)
                dve.wait_ge(cb_mask, c + 1)
                for s in range(8):
                    k = 8 * c + s
                    dve.wait_ge(seg_exp, k + 1)
                    if k >= 2:
                        dve.wait_ge(y_prod, k - 1)
                    nc.vector.tensor_tensor(MM[:, k % 2, :, :], EE[:, k % 2, :, :],
                                            CBM[:, s // 2, :][:, None, :].to_broadcast([P, 3, P]), ALU.mult)\
                        .then_inc(seg_m, 1)
                    if s % 2:
                        g = s // 2
                        dve.wait_ge(off_prod, 4 * c + g + 1)
                        nc.vector.tensor_tensor(heads(YO, GW * g), heads(M[:, (g + 1) % 2, :]),
                                                per_head(24 * c, g), ALU.mult).then_inc(off_done, 1)
                if c == 0:
                    for g in range(SSD_G):
                        dve.wait_ge(off_prod, 4)
                        step(nc.vector.tensor_tensor(heads(ST, GW * g), heads(ST, GW * g), per_head(72, g), ALU.mult))
                    step.wait()
                    for g in range(SSD_G):
                        dve.wait_ge(st_prod, SSD_G + g + 1)
                        nc.vector.tensor_tensor(ST[:, GW * g:GW * g + GW], ST[:, GW * g:GW * g + GW],
                                                M[:, g % 2, 0:GW], ALU.add).then_inc(st_done, 1)
                dve.wait_ge(y_prod, 8 * c + 8)
                dve.wait_ge(off_done, 4 * c + 4)
                yd = Y[:, :, :].rearrange("p a b -> p (a b)")[:, 0:D_SSD]
                nc.vector.tensor_tensor(YO[:, :], YO[:, :], yd, ALU.add).then_inc(y_add, 1)
                dve.wait_ge(y_add, 2 * c + 1)
                dve.wait_ge(xd_done, c + 1)
                nc.vector.tensor_tensor(YO[:, :], YO[:, :], XT[:, c + 1, :], ALU.add).then_inc(y_add, 1)
                dve.wait_ge(y_add, 2 * c + 2)
                dve.wait_ge(z_out, 3)
                nc.vector.tensor_tensor(YO[:, :], YO[:, :], Z[:, c, :], ALU.mult).then_inc(y_gate, 1)
                dve.wait_ge(grp_rstd, c + 1)
                for g in range(SSD_G):
                    nc.vector.scalar_tensor_tensor(
                        out=YO[:, GW * g:GW * g + GW], in0=YO[:, GW * g:GW * g + GW], scalar=stat[:, 28 + g:29 + g],
                        in1=rowp[:, ROW["ssd_norm"] + GW * g:ROW["ssd_norm"] + GW * g + GW],
                        op0=ALU.mult, op1=ALU.mult).then_inc(grp_y, 1)
                for q in range(3):
                    dve.wait_ge(y_hi, 3 * c + q + 1)
                    nc.vector.tensor_tensor(m2l[:, 4 * q:4 * q + 4, P * c:P * c + P],
                                            M[:, (3 * c + q) % 2, :].rearrange("p (k t) -> p k t", k=4),
                                            m2h[:, 4 * q:4 * q + 4, P * c:P * c + P].bitcast(F32), ALU.subtract)\
                        .then_inc(y_lo, 1)
            split_ahead(STREAM["wout2"], 16)
            for j in range(TT):
                dve.wait_ge(w_used, LAST["wout2"])
                nc.vector.tensor_tensor(X[:, j, :], X[:, j, :], Y[:, j, :], ALU.add).then_inc(x_ready, 1)
            norm(5)
            with dve.Fori(0, 4) as i:
                for j in range(4):
                    split(STREAM["wq"] + 4, j, i)

            def best16(n, vals, rest, top, pos, index):
                for k in range(n):
                    step(nc.vector.max(top(k)[:, 0:8], vals(k)))
                step.wait()
                for k in range(n):
                    step(nc.vector.max_index(pos(k)[:, 0:8], top(k)[:, 0:8], vals(k)))
                    step(nc.vector.match_replace(rest(k), top(k)[:, 0:8], vals(k), 3 * NEG))
                step.wait()
                for k in range(n):
                    step(nc.vector.max(top(k)[:, 8:16], rest(k)))
                step.wait()
                for k in range(n):
                    step(nc.vector.max_index(pos(k)[:, 8:16], top(k)[:, 8:16], rest(k)))
                step.wait()

            for j in range(TT):
                dve.wait_ge(s_out, 4 * j + 4)
                best16(16, lambda k: SCO[:, j, k, :], lambda k: SCO2[:, k, :], lambda k: V16[:, k, :],
                       lambda k: I16[:, k, :], None)
                step(nc.vector.tensor_copy(I16F[:, :, :], I16[:, :, :]))
                for h in range(PEER_H):
                    step(nc.vector.tensor_tensor(
                        cand[:, h, :].rearrange("p (a b) -> p a b", a=TOPK),
                        V16[:, 2 * h, :][:, :, None].to_broadcast([P, TOPK, TOPK]),
                        V16[:, 2 * h + 1, :][:, None, :].to_broadcast([P, TOPK, TOPK]), ALU.add))
                step.wait()
                if j:
                    dve.wait_ge(top_nat, 1)
                best16(8, lambda h: cand[:, h, :], lambda h: cand2[:, h, :], lambda h: BV[:, h, :],
                       lambda h: PU[:, h, :], None)
                step(nc.vector.tensor_scalar(PA[:, 0, :], PU[:, :, :].rearrange("p h k -> p (h k)"), 4, None,
                                             ALU.logical_shift_right))
                step(nc.vector.tensor_scalar(PA[:, 1, :], PU[:, :, :].rearrange("p h k -> p (h k)"), 15, None,
                                             ALU.bitwise_and))
                nc.vector.tensor_tensor(cand[:, :, 0:TOPK], BV[:, :, :],
                                        BV[:, :, 0:1].to_broadcast([P, PEER_H, TOPK]), ALU.subtract)\
                    .then_inc(top_sub_own, 1)
                dve.wait_ge(top_sub_own, j + 1)
                nc.vector.tensor_copy(BV[:, :, :], cand[:, :, 0:TOPK]).then_inc(top_sub, 1)
                step.wait()
                step(nc.vector.tensor_copy(PF[:, :, :], PA[:, :, :]))
                step.wait()
                for half in range(2):
                    step.wait()
                    step(nc.vector.tensor_tensor(eqs[:, :, :], PF[:, half, :][:, :, None].to_broadcast([P, HK, TOPK]),
                                                 iota[:, 0:TOPK][:, None, :].to_broadcast([P, HK, TOPK]),
                                                 ALU.is_equal))
                    step.wait()
                    for h in range(PEER_H):
                        e = eqs[:, TOPK * h:TOPK * h + TOPK, :]
                        step(nc.vector.tensor_tensor(
                            e, e, I16F[:, 2 * h + half, :][:, None, :].to_broadcast([P, TOPK, TOPK]), ALU.mult))
                    step.wait()
                    if j and not half:
                        dve.wait_ge(top_turn, j)
                    step(nc.vector.tensor_reduce(NAT[:, half, :], eqs[:, :, :], AX_X, ALU.add))
                dve.wait_ge(top_exp, j + 1)
                step(nc.vector.tensor_reduce(gsum[:, 0:PEER_H], BV[:, :, :], AX_X, ALU.add))
                step.wait()
                step(nc.vector.reciprocal(gsum[:, PEER_H:], gsum[:, 0:PEER_H]))
                step.wait()
                nc.vector.tensor_tensor(NAT[:, 2, :].rearrange("p (h k) -> p h k", h=PEER_H), BV[:, :, :],
                                        gsum[:, PEER_H:][:, :, None].to_broadcast([P, PEER_H, TOPK]), ALU.mult)\
                    .then_inc(top_nat, 1)

            dve.wait_ge(top_T, TT)
            dve.wait_ge(spilled, 16)
            dve.wait_ge(norm_scaled, sum(NORM_TILES))

            def hot(i, s):
                for t in range(4):
                    ins = nc.vector.tensor_scalar(hotB[:, s, t, :], iota[:, :], i1T[:, bass.ds(i * 8 + 4 * s + t, 1)],
                                                  gT[:, bass.ds(i * 8 + 4 * s + t, 1)], ALU.is_equal, ALU.mult)
                ins.then_inc(hot_b, 1)
                nc.vector.tensor_tensor(hotA[:, s, :, :],
                                        i2T[:, bass.ds(i * 8 + 4 * s, 4)][:, :, None].to_broadcast([P, 4, KEYS]),
                                        iota[:, None, :].to_broadcast([P, 4, KEYS]), ALU.is_equal).then_inc(hot_a, 1)

            for s in range(2):
                hot(0, s)
            with dve.Fori(1, T // 8) as i:
                for s in range(2):
                    dve.wait_ge(g_prod, i * 2 + s - 1)
                    hot(i, s)
            dve.wait_ge(g_out, T // 4)
            mlp("peer", KEYS, peer_hid, peer_act, peer_ah, peer_al, weighed, A_BASE["peer"], FF_CHUNKS)
            dve.wait_ge(w_used, N_BLOCKS)
            dve.wait_ge(fin_in, 32)
            for j in range(TT):
                nc.vector.tensor_tensor(fin_t[:, j, :], fin_x[:, j, :], Y[:, j, :], ALU.add).then_inc(fin_y, 1)
            for j in range(TT):
                dve.wait_ge(fin_rstd, j + 1)
                nc.vector.scalar_tensor_tensor(out=fin_x[:, j, :], in0=fin_t[:, j, :], scalar=stat[:, 12 + j:13 + j],
                                               in1=fin_g[:, :], op0=ALU.mult, op1=ALU.mult).then_inc(fin_y, 1)

        @block.gpsimd
        def _(pool):
            step = Steps(pool, pool_step)
            nc.gpsimd.memset(ones[:, :], 1.0).then_inc(consts, 1)
            nc.gpsimd.memset(ident[:, :], 0.0).then_inc(consts, 1)
            nc.gpsimd.memset(mask[:, :], 0.0).then_inc(consts, 1)
            nc.gpsimd.memset(neg_half[:, :], -0.5).then_inc(consts, 1)
            nc.gpsimd.iota(iota[:, :], [[1, P]], base=0, channel_multiplier=0,
                           allow_small_or_imprecise_dtypes=True).then_inc(consts, 1)
            pool.wait_ge(consts, 5)
            nc.gpsimd.affine_select(out=ident[:, :], in_=ident[:, :], pattern=[[-1, P]], compare_op=ALU.not_equal,
                                    fill=1.0, base=0, channel_multiplier=1).then_inc(consts, 1)
            nc.gpsimd.affine_select(out=upper[:, :], in_=ones[:, :], pattern=[[1, P]], compare_op=ALU.is_ge,
                                    fill=0.0, base=0, channel_multiplier=-1).then_inc(consts, 1)
            nc.gpsimd.affine_select(out=later[:, :], in_=ones[:, :], pattern=[[-1, P]], compare_op=ALU.is_gt,
                                    fill=0.0, base=0, channel_multiplier=1).then_inc(consts, 1)
            nc.gpsimd.affine_select(out=mask[:, P:], in_=mask[:, P:], pattern=[[-1, P]], compare_op=ALU.is_ge,
                                    fill=NEG, base=0, channel_multiplier=1).then_inc(consts, 1)

            def inverse_root(dst, src, n, done):
                step(nc.gpsimd.tensor_scalar(dst, src, 1.0 / n, EPS, ALU.mult, ALU.add))
                step.wait()
                nc.gpsimd.tensor_tensor(dst, dst, neg_half[0:dst.shape[0], :].to_broadcast(list(dst.shape)), ALU.pow)\
                    .then_inc(done, 1)

            def norm(n):
                tiles, _, _ = pieces(n)
                t0 = sum(NORM_TILES[:n])
                for k, (_, r, _) in enumerate(tiles):
                    pool.wait_ge(norm_ss, t0 + k + 1)
                    inverse_root(stat[0:r, 8 + k:9 + k], stat[0:r, k:k + 1], D, norm_rstd)

            def post(p):
                for j in range(TT):
                    pool.wait_ge(post_ss, 2 * p + j + 1)
                    inverse_root(stat[:, 12 + j:13 + j], stat[:, 4 + j:5 + j], D, post_rstd)

            norm(0)
            pool.wait_ge(consts, 9)
            pool.wait_ge(logf, 1)
            zf = SQ[:, 0, 0:16].rearrange("p (j h) -> p j h", j=TT)
            for n, (j, m) in enumerate(((0, later), (1, ones), (1, later))):
                nc.gpsimd.tensor_tensor(DEC[:, :, n, :], zf[:, j, :][:, :, None].to_broadcast([P, FOX_H, P]),
                                        m[:, None, :].to_broadcast([P, FOX_H, P]), ALU.mult).then_inc(dec_done, 1)
            norm(1)
            pool.wait_ge(ln_var, 1)
            v = UP[:, 0, 0:T]
            nc.gpsimd.tensor_tensor(v, v, neg_half[:, :].to_broadcast([P, T]), ALU.pow).then_inc(ln_rstd, 1)
            for p in range(3):
                post(p)
                norm(2 + p)
            pool.wait_ge(a_free, A_BASE["sc"] + 12)
            step(nc.gpsimd.memset(SP[:, :, 0:2], 0.0))
            step(nc.gpsimd.tensor_tensor(SP[:, :, 2:], SCX[:, SC_T:2 * SC_T, :], SCX[:, 2 * SC_T:, :], ALU.mult))
            step.wait()
            for k in range(SC_T):
                t0, t1 = sct[:, k % 2, :], SP_tmp[:, :]

                def tap(w):
                    return SP[:, k, META + w:META + w + T], colp[:, COL["sc_w"] + 3 * k + w:COL["sc_w"] + 3 * k + w + 1]

                if k >= 2:
                    pool.wait_ge(sc_lo, k - 1)
                a, wt = tap(0)
                step(nc.gpsimd.tensor_scalar(t0, a, wt, None, ALU.mult))
                for w in (1, 2):
                    a, wt = tap(w)
                    step(nc.gpsimd.tensor_scalar(t1, a, wt, None, ALU.mult))
                    step.wait()
                    step(nc.gpsimd.tensor_tensor(t0, t0, t1, ALU.add))
                    step.wait()
                nc.gpsimd.tensor_tensor(t0, t0, SCX[:, k, META:], ALU.mult).then_inc(sc_y, 1)
            pool.wait_ge(sc_lo, SC_T)

            def bc(t, r, w=SSD_D):
                return t[:, :, None].to_broadcast([r, SSD_H, w])

            def spread_xdd(c):
                r = META if c == 0 else P
                o = 96 if c == 0 else 48
                nc.gpsimd.tensor_tensor(XDD[0:r, :].rearrange("p (h d) -> p h d", h=SSD_H),
                                        XT[0:r, c, :].rearrange("p (h d) -> p h d", h=SSD_H),
                                        bc(exs[0:r, o:o + 24], r), ALU.mult).then_inc(xdd_done, 1)

            pool.wait_ge(tr_out, 3)
            pool.wait_ge(xdd_w, 2)
            spread_xdd(0)
            pool.wait_ge(tr_out, 11)

            def decay_inputs(k):
                c, s = divmod(k, 8)
                if k >= 2:
                    pool.wait_ge(seg_prod, k - 1)
                a = dtz[:, 3, 24 * (c + 1) + 3 * s:24 * (c + 1) + 3 * s + 3]
                nc.gpsimd.tensor_tensor(AU[:, k % 2, :, :], a[:, :, None].to_broadcast([P, 3, P]),
                                        upper[:, None, :].to_broadcast([P, 3, P]), ALU.mult).then_inc(au_done, 1)

            def spread_xdt(c):
                nc.gpsimd.tensor_tensor(XDT[:, c, :].rearrange("p (h d) -> p h d", h=SSD_H),
                                        XT[:, c + 1, :].rearrange("p (h d) -> p h d", h=SSD_H),
                                        bc(dtz[:, 2, 24 * (c + 1):24 * (c + 2)], P), ALU.mult).then_inc(xdt_done, 1)

            def skip(c):
                nc.gpsimd.tensor_tensor(XT[:, c + 1, :].rearrange("p (h d) -> p h d", h=SSD_H),
                                        XT[:, c + 1, :].rearrange("p (h d) -> p h d", h=SSD_H),
                                        bc(rowp[:, ROW["d_skip"]:ROW["d_skip"] + SSD_H], P), ALU.mult)\
                    .then_inc(xd_done, 1)

            def group_norm(c):
                pool.wait_ge(grp_ss, 4 * c + 4)
                inverse_root(stat[:, 28:32], stat[:, 24:28], GW, grp_rstd)

            decay_inputs(0)
            decay_inputs(1)
            spread_xdt(0)
            for k in range(2, 4):
                decay_inputs(k)
            pool.wait_ge(st_prod, SSD_G)
            spread_xdd(1)
            pool.wait_ge(xdt_done, 1)
            pool.wait_ge(xdd_done, 2)
            for k in range(4, 8):
                decay_inputs(k)
            skip(0)
            spread_xdt(1)
            pool.wait_ge(xdt_done, 2)
            for k in range(8, 10):
                decay_inputs(k)
            group_norm(0)
            for k in range(10, 12):
                decay_inputs(k)
            skip(1)
            for k in range(12, 16):
                decay_inputs(k)
            group_norm(1)
            pool.wait_ge(w_used, STREAM["wout2"] + 1)
            pool.wait_ge(grp_y, 8)
            pool.dma_start(keys[:, :, :], keys_in).then_inc(keys_land, 16)
            pool.wait_ge(x_ready, 8)
            pool.dma_start(h2_spill, X[:, :, :]).then_inc(spilled, 16)
            norm(5)
            for j in range(TT):
                pool.wait_ge(fin_ss, j + 1)
                inverse_root(stat[:, 12 + j:13 + j], stat[:, 4 + j:5 + j], D, fin_rstd)

        @block.tensor
        def _(pe):
            def mm(o, a, b, start, stop):
                return nc.tensor.matmul(o, a, b, start=start, stop=stop)

            def wide(name, j, rh, rl, n, i=0):
                b = STREAM[name] + j
                e = A_BASE[name] + j
                s = b % SLOTS
                pe.wait_ge(split_lo, i * 4 + (b + 1))
                if not (type(i) is int and 4 * i + e < 2):
                    pe.wait_ge(a_free, i * 4 + (e - 1))
                wide_products(s, e % 2, rh, rl, n).then_inc(w_used, 1)

            def wide_products(s, bank, rh, rl, n):
                for kt in range(KT):
                    h, l = wh[:, s, P * kt:P * kt + P], wl[:, s, P * kt:P * kt + P]
                    mm(AO[:, bank, 0:n], h, rh[:, kt, 0:n], kt == 0, False)
                    mm(AO[:, bank, 0:n], h, rl[:, kt, 0:n], False, False)
                    ins = mm(AO[:, bank, 0:n], l, rh[:, kt, 0:n], False, kt == KT - 1)
                return ins

            def flat(s, outs, ah, al, offs, first, last):
                for j in range(TT):
                    for n, o in enumerate(offs):
                        mm(outs[j][n], ah[j], wh[:, s, o:o + 512], first, False)
                        mm(outs[j][n], ah[j], wl[:, s, o:o + 512], False, False)
                        ins = mm(outs[j][n], al[j], wh[:, s, o:o + 512], False, last)
                return ins

            Y4 = [[Y[:, j, 0:512], Y[:, j, 512:1024]] for j in range(TT)]

            def flat_stage(name, n, ah, al):
                for kt in range(n):
                    b = STREAM[name] + kt
                    pe.wait_ge(split_lo, b + 1)
                    flat(b % SLOTS, Y4, [ah[:, kt, P * j:P * j + P] for j in range(TT)],
                         [al[:, kt, P * j:P * j + P] for j in range(TT)], (0, 512), kt == 0, kt == n - 1)\
                        .then_inc(w_used, 1)

            def half_stage(b0, half, ah, al, c0):
                for k in range(4):
                    pe.wait_ge(split_lo, b0 + k + 1)
                    for q in range(2):
                        kt = 2 * k + q
                        ins = flat((b0 + k) % SLOTS, [[Y4[half][j]] for j in range(TT)],
                                   [ah[:, kt, c0 + P * j:c0 + P * j + P] for j in range(TT)],
                                   [al[:, kt, c0 + P * j:c0 + P * j + P] for j in range(TT)],
                                   (512 * q,), kt == 0, kt == KT - 1)
                    ins.then_inc(w_used, 1)

            def norm(n):
                tiles, dh, dl = pieces(n)
                t0 = sum(NORM_TILES[:n])
                for k, (src, r, c) in enumerate(tiles):
                    pe.wait_ge(norm_scaled, t0 + k + 1)
                    for q in range(2):
                        g = 2 * (t0 + k) + q
                        if g >= 2:
                            pe.wait_ge(norm_lo, g - 1)
                        for i in range(4):
                            kt = 4 * q + i
                            ins = nc.tensor.transpose(M[:, g % 2, P * i:P * i + r], xn[0:r, k, P * kt:P * kt + P],
                                                      ident[0:r, 0:r])
                        ins.then_inc(norm_turned, 1)
                pe.wait_ge(norm_lo, 2 * (t0 + len(tiles)))

            def thin(outs, w, width):
                for o, r, c in outs:
                    for kt in range(KT):
                        for n, part in enumerate((xh, xl)):
                            ins = mm(o, part[:, kt, c:c + r].bitcast(F32), w[:, width * kt:width * kt + width],
                                     kt == 0 and n == 0, kt == KT - 1 and n == 1)
                return ins

            pe.wait_ge(consts, 9)
            norm(0)
            for j in range(8):
                wide("ag", j, xh, xl, T)
            for j in range(8):
                wide("qk", j, xh, xl, T)
            half_stage(STREAM["v"], 0, xh, xl, 0)
            thin([(M[:, 0, 8 * j:8 * j + 8], P, P * j) for j in range(TT)],
                 colp[:, COL["w_f"]:COL["w_f"] + KT * FOX_H], FOX_H).then_inc(f_prod, 1)
            pe.wait_ge(logf, 1)
            norm(1)
            for j in range(4):
                wide("mk", j, mh, ml, T)
            half_stage(STREAM["mv"], 1, mh, ml, 0)
            pe.wait_ge(conv_done, 1)
            for c in range(CT):
                ins = mm(M[:, 0, 0:T], ones[:, :], CV[:, c, :], c == 0, c == CT - 1)
            ins.then_inc(ln_sum, 1)
            pe.wait_ge(ln_sq, 1)
            for c in range(CT):
                ins = mm(M[:, 1, 0:T], ones[:, :], SQ[:, c, :], c == 0, c == CT - 1)
            ins.then_inc(ln_sum, 1)
            pe.wait_ge(ln_y, 1)
            pe.wait_ge(dec_done, 3)
            pe.wait_ge(v_out, 1)
            pe.wait_ge(mv_out, 1)

            def attention(first, last):
                for s in range(first, last + 3):
                    u = s
                    if u < last:
                        kind, h, j = units[u]
                        o = M[:, u % 2, :]
                        if u >= 2:
                            pe.wait_ge(at_max, u - 1)
                        if kind == "fox":
                            r = slice(FOX_D * (h % 2), FOX_D * (h % 2) + FOX_D)
                            q, k = QK[r, h // 2, P * j:P * j + P], QK[r, CT + h // 2, 0:P * (j + 1)]
                            mm(o[:, 0:P * (j + 1)], q, k, True, False)
                            if j == 0:
                                ins = mm(o[:, 0:P], upper[:, :], DEC[:, h, 0, :], False, True)
                            else:
                                mm(o[:, 0:P], ones[:, :], DEC[:, h, 0, :], False, False)
                                ins = mm(o[:, 0:2 * P], upper[:, :],
                                         DEC[:, h, 1:3, :].rearrange("p a b -> p (a b)"), False, True)
                        else:
                            ins = mm(o[:, 0:T], MQ[:, h, P * j:P * j + P], MK[:, h, :], True, True)
                        ins.then_inc(at_logit, 1)
                    u = s - 2
                    if first <= u < last:
                        pe.wait_ge(at_p, u + 1)
                        if u >= 2:
                            pe.wait_ge(at_pt, u - 1)
                        for kt in range(unit_keys(u) // P):
                            ins = nc.tensor.transpose(Y[:, 0, 512 * (u % 2) + P * kt:512 * (u % 2) + P * kt + P],
                                                      att_p[:, u % 2, P * kt:P * kt + P], ident[:, :])
                        ins.then_inc(at_turn, 1)
                    u = s - 3
                    if first <= u < last:
                        kind, h, j = units[u]
                        pe.wait_ge(at_pt, u + 1)
                        if u >= 2:
                            pe.wait_ge(at_lo, u - 1)
                        n = unit_keys(u) // P
                        vals, v = (V, h // 2) if kind == "fox" else (MV, h)
                        for kt in range(n):
                            ins = mm(Y[:, 1, 512 * (u % 2):512 * (u % 2) + P], vals[:, kt, P * v:P * v + P],
                                     att_pt[:, u % 2, kt, :], kt == 0, kt == n - 1)
                        ins.then_inc(at_pv, 1)

            attention(0, fox_units)
            pe.wait_ge(at_lo, fox_units)
            pe.wait_ge(ln_lo, 1)
            flat_stage("wout", 8, mixh, mixl)
            norm(2)
            for j in range(4):
                wide("mq", j, xh, xl, T)
            pe.wait_ge(a_free, A_BASE["mq"] + 4)
            attention(fox_units, len(units))
            pe.wait_ge(at_lo, len(units))
            flat_stage("mo", 4, moh, mol)
            norm(3)

            def mlp(name, n, ah, al, base):
                b0 = STREAM[name]

                def up(s, i, bank):
                    b = b0 + 2 * s - 1
                    pe.wait_ge(split_lo, i * 4 + (b + 1))
                    pe.wait_ge(a_free, i * 2 + (A_BASE[name] + s - 1))
                    wide_products(b % SLOTS, bank, xh, xl, T).then_inc(w_used, 1)

                def down(b, s, i, first, last):
                    pe.wait_ge(split_lo, i * 4 + (b + 1))
                    pe.wait_ge(hid_lo, i * 2 + (base + s + 1))
                    flat(b % SLOTS, Y4, [ah[:, s, P * j:P * j + P] for j in range(TT)],
                         [al[:, s, P * j:P * j + P] for j in range(TT)], (0, 512), first, last).then_inc(w_used, 1)

                pe.wait_ge(split_lo, b0 + 1)
                wide_products(b0 % SLOTS, A_BASE[name] % 2, xh, xl, T).then_inc(w_used, 1)
                for s in range(2):
                    up(s + 1, 0, (s + 1) % 2)
                    down(b0 + 2 + 2 * s, s, 0, s == 0, False)
                with pe.Fori(1, n // 2 - 1) as i:
                    for s in range(2):
                        up(s + 1, i, (s + 1) % 2)
                        down(b0 + 2 + 2 * s, s, i, False, False)
                i = n // 2 - 1
                up(1, i, 1)
                down(b0 + 2, 0, i, False, False)
                down(down_block(b0, n - 1, n) - 4 * i, 1, i, False, True)

            mlp("mlp", FF_CHUNKS, mlp_ah, mlp_al, 0)
            norm(4)
            thin([(M[0:META, 0, 0:24], META, 0)] + [(M[:, 0, 24 * (j + 1):24 * (j + 2)], P, META + P * j)
                                                    for j in range(TT)],
                 colp[:, COL["w_dt"]:COL["w_dt"] + KT * SSD_H], SSD_H).then_inc(dt_prod, 1)
            with pe.Fori(0, XBC_T // 4) as i:
                for j in range(4):
                    wide("xbc", j, xh, xl, TM, i)
            with pe.Fori(0, SC_T * 3 // 4) as i:
                for j in range(4):
                    wide("sc", j, xh, xl, TM, i)
            pe.wait_ge(x_ready, 6)
            for g in range(3):
                if g == 2:
                    pe.wait_ge(z_out, 1)
                half_stage(STREAM["z"] + 4 * g, g % 2, xh, xl, META)
            pe.wait_ge(xsilu, XBC_T // 4)
            pe.wait_ge(dt_a, 2)
            n_tr = 0
            for c in range(3):
                r = META if c == 0 else P
                t0 = 0 if c == 0 else META + P * (c - 1)
                for q in range(4 if c < 2 else 3):
                    if n_tr >= 2:
                        pe.wait_ge(tr_out, n_tr - 1)
                    for i in range(4):
                        ins = nc.tensor.transpose(M[0:r, n_tr % 2, P * i:P * i + P], XS[:, 4 * q + i, t0:t0 + r],
                                                  ident[:, :])
                    ins.then_inc(tr_in, 1)
                    n_tr += 1
            pe.wait_ge(a_free, A_BASE["sc"] + 12)
            a1, a2, a0 = dtz[:, 3, 24:48], dtz[:, 3, 48:72], dtz[0:META, 3, 0:24]
            mm(AO[:, 1, 0:24], upper[:, :], a1, True, True)
            mm(AO[:, 1, 24:48], upper[:, :], a2, True, True)
            mm(AO[:, 1, 48:72], later[:, :], a1, True, True)
            mm(AO[:, 1, 72:96], ones[:, :], a1, True, True)
            mm(AO[0:META, 1, 96:120], later[0:META, 0:META], a0, True, True).then_inc(ac_prod, 1)
            pe.wait_ge(tr_out, 11)
            pe.wait_ge(xdd_done, 1)
            for g in range(SSD_G):
                if g >= 2:
                    pe.wait_ge(st_done, g - 1)
                mm(M[:, g % 2, 0:GW], BN[0:META, 0, P * g:P * g + P], XDD[0:META, GW * g:GW * g + GW], True, True)\
                    .then_inc(st_prod, 1)
            pe.wait_ge(st_done, SSD_G)
            pe.wait_ge(z_out, 3)
            for c in range(TT):
                tok = slice(META + P * c, META + P * c + P)
                if c:
                    pe.wait_ge(y_lo, 3)
                for g in range(SSD_G):
                    ins = mm(M[:, 0, P * g:P * g + P], XS[:, XS_T + g, tok], XS[:, XS_T + SSD_G + g, tok], True, True)
                ins.then_inc(cb_prod, 1)
                pe.wait_ge(xdt_done, c + 1)
                if c:
                    pe.wait_ge(st_done, 2 * SSD_G)

                def seg(s):
                    k = 8 * c + s
                    pe.wait_ge(au_done, k + 1)
                    if k < 2:
                        pe.wait_ge(ac_exp, 2)
                    else:
                        pe.wait_ge(seg_exp, k - 1)
                    mm(AO[:, k % 2, 0:3 * P], later[:, :], AU[:, k % 2, :, :].rearrange("p a b -> p (a b)"),
                       True, True).then_inc(seg_prod, 1)

                seg(0)
                for s in range(8):
                    if s < 7:
                        seg(s + 1)
                    if s % 2 == 0:
                        g = s // 2
                        if g == 0:
                            pe.wait_ge(cb_mask, c + 1)
                        else:
                            pe.wait_ge(off_done, 4 * c + g - 1) if 4 * c + g - 1 > 0 else None
                        mm(M[:, (g + 1) % 2, 0:GW], XS[:, XS_T + SSD_G + g, tok], ST[:, GW * g:GW * g + GW],
                           True, True).then_inc(off_prod, 1)
                    k = 8 * c + s
                    pe.wait_ge(seg_m, k + 1)
                    yd = Y[:, :, :].rearrange("p a b -> p (a b)")
                    for t in range(3):
                        h = 3 * s + t
                        ins = mm(yd[:, SSD_D * h:SSD_D * h + SSD_D], MM[:, k % 2, t, :],
                                 XDT[:, c, SSD_D * h:SSD_D * h + SSD_D], True, True)
                    ins.then_inc(y_prod, 1)
                if c == 0:
                    pe.wait_ge(xdd_done, 2)
                    pe.wait_ge(off_done, 4)
                    for g in range(SSD_G):
                        if g >= 2:
                            pe.wait_ge(st_done, SSD_G + g - 1)
                        mm(M[:, g % 2, 0:GW], BN[:, 1, P * g:P * g + P], XDD[:, GW * g:GW * g + GW], True, True)\
                            .then_inc(st_prod, 1)
                    pe.wait_ge(st_done, 2 * SSD_G)
                pe.wait_ge(grp_y, 4 * c + 4)
                for q in range(3):
                    k = 3 * c + q
                    if k >= 2:
                        pe.wait_ge(y_lo, k - 1)
                    for i in range(4):
                        ins = nc.tensor.transpose(M[:, k % 2, P * i:P * i + P],
                                                  YO[:, P * (4 * q + i):P * (4 * q + i) + P], ident[:, :])
                    ins.then_inc(y_turn, 1)
            pe.wait_ge(y_lo, 6)
            pe.wait_ge(sc_lo, SC_T)
            flat_stage("wout2", 16, m2h, m2l)
            norm(5)
            with pe.Fori(0, 4) as i:
                for j in range(4):
                    wide("wq", j, xh, xl, T, i)
            pe.wait_ge(a_free, A_BASE["wq"] + 16)
            pe.wait_ge(keys_land, 16)
            for q in range(8):
                j = q // 4
                if q >= 4:
                    pe.wait_ge(s_out, q - 3)
                for n in range(4):
                    hs = 4 * (q % 4) + n
                    ins = mm(Y[:, (q // 2) % 2, 512 * (q % 2) + P * n:512 * (q % 2) + P * n + P],
                             QP[:, hs, P * j:P * j + P], keys[:, hs, :], True, True)
                ins.then_inc(s_prod, 1)
            for j in range(TT):
                pe.wait_ge(top_nat, j + 1)
                for n in range(3):
                    ins = nc.tensor.transpose(M[:, j, P * n:P * n + P], NAT[:, n, :], ident[:, :])
                ins.then_inc(top_turn, 1)
            pe.wait_ge(top_T, TT)

            def spread(i, s):
                pe.wait_ge(hot_a, i * 2 + s + 1)
                pe.wait_ge(hot_b, i * 2 + s + 1)
                for t in range(4):
                    ins = mm(M[:, s, P * t:P * t + P], hotA[:, s, t, :], hotB[:, s, t, :], True, True)
                ins.then_inc(g_prod, 1)

            for s in range(2):
                spread(0, s)
            with pe.Fori(1, T // 8) as i:
                for s in range(2):
                    pe.wait_ge(g_out, i * 2 + s - 1)
                    spread(i, s)
            pe.wait_ge(s_out, 8)
            mlp("peer", KEYS, peer_ah, peer_al, FF_CHUNKS)


def kernel(**inputs):
    import concourse.bacc as _bacc
    from concourse.bass_utils import run_bass_kernel_spmd as _run

    a = {k: np.asarray(v) for k, v in inputs.items()}

    def wide_blocks(w):
        return w.reshape(KT, P, -1, P).transpose(2, 1, 0, 3).reshape(-1, P, BLK)

    def flat_blocks(w):
        return w.reshape(-1, P, BLK)

    def half_blocks(w):
        return w.reshape(4, 2, P, 512).transpose(0, 2, 1, 3).reshape(-1, P, BLK)

    def mlp_blocks(up, down):
        u, d = wide_blocks(up), flat_blocks(down)
        n = len(u)
        order = [u[0:1]]
        for c in range(n - 1):
            order += [u[c + 1:c + 2], d[c:c + 1]]
        return np.concatenate(order + [d[n - 1:n]])

    w_in, w2 = a["w_in"][0], a["w_in_2"][0]
    c1, c2, c3, c4 = CONV_CH * 2, CONV_CH * 2 + 1024, CONV_CH * 2 + 1536, w_in.shape[1]
    z1, z2, z3 = D_SSD, D_SSD + XBC_T * P, D_SSD + XBC_T * P + SSD_H
    stream = np.concatenate([
        wide_blocks(w_in[:, 0:c1]), wide_blocks(w_in[:, c1:c2]), half_blocks(w_in[:, c2:c3]),
        wide_blocks(a["w_mk"][0]), half_blocks(a["w_mv"][0]), flat_blocks(a["w_out"][0]),
        wide_blocks(a["w_mq"][0]), flat_blocks(a["w_mo"][0]), mlp_blocks(a["w_up"][0], a["w_down"][0]),
        wide_blocks(w2[:, z1:z2]), wide_blocks(w2[:, z3:]),
        *[half_blocks(w2[:, 512 * g:512 * g + 512]) for g in range(3)], flat_blocks(a["w_out_2"][0]),
        wide_blocks(a["w_q_2"][0]), mlp_blocks(a["expert_u_2"][0].T, a["expert_v_2"][0])])
    assert stream.shape == (N_BLOCKS, P, BLK)

    def on_partitions(v, n):
        v = v.reshape(-1, n, P)
        return v.transpose(2, 1, 0).reshape(P, -1)

    gain_cols = np.concatenate([on_partitions(a[k], KT) for k in (
        "norm_mix_pre", "norm_memkv", "norm_mem_pre", "norm_mlp_pre", "g_mix_2", "g_ffn_2")], 1)
    cols = np.concatenate([
        on_partitions(a["conv_w"][0], CT), on_partitions(a["conv_b"], CT), on_partitions(a["conv_ln_g"], CT),
        on_partitions(a["conv_ln_b"], CT), on_partitions(a["conv_ssd_w_2"][0], XBC_T),
        on_partitions(a["conv_ssd_b_2"], XBC_T), on_partitions(a["conv_sc_w_2"][0], SC_T),
        w_in[:, c3:c4].reshape(KT, P, FOX_H).transpose(1, 0, 2).reshape(P, -1),
        w2[:, z2:z3].reshape(KT, P, SSD_H).transpose(1, 0, 2).reshape(P, -1)], 1)
    rows = np.concatenate([a[k].reshape(-1) for k in ("b_forget", "dt_bias_2", "a_log_2", "d_skip_2", "ssd_norm_w_2")])
    post = np.stack([a[k].reshape(-1) for k in ("norm_mix_post", "norm_mem_post", "norm_mlp_post", "g_final_2")])
    keys_in = a["sub_keys_2"][0].reshape(16, KEYS, P).transpose(2, 0, 1)
    arrays = {
        "in_stream": stream, "in_gains": gain_cols, "in_cols": cols, "in_rows": rows, "in_post": post,
        "in_x": a["x"][0].reshape(TT, P, D).transpose(1, 0, 2), "in_mem": a["mem"][0].reshape(TT, P, D).transpose(1, 0, 2),
        "in_meta": a["meta_tokens_2"], "in_keys": keys_in,
    }
    arrays = {k: np.ascontiguousarray(v) for k, v in arrays.items()}
    nc = _bacc.Bacc("TRN2", target_bir_lowering=False, num_devices=1)
    ap = {k: nc.dram_tensor(k, v.shape, F32, kind="ExternalInput").ap() for k, v in arrays.items()}
    out = nc.dram_tensor("out_x", (P, TT, D), F32, kind="ExternalOutput").ap()
    spill = nc.dram_tensor("h2_spill", (P, TT, D), F32).ap()
    build(nc, ap["in_stream"], ap["in_gains"], ap["in_cols"], ap["in_rows"], ap["in_post"], ap["in_x"],
          ap["in_mem"], ap["in_meta"], ap["in_keys"], out, spill)
    r = _run(nc, [arrays], core_ids=[0])
    got = r.results[0]["out_x"]
    return np.ascontiguousarray(got.transpose(1, 0, 2).reshape(1, T, D))
```

```python
from contextlib import ExitStack

import numpy as np

import concourse.bass as bass
from concourse import mybir

P = 128
F32 = mybir.dt.float32
F32R = mybir.dt.float32r
U32 = mybir.dt.uint32
BF16 = mybir.dt.bfloat16
ACT = mybir.ActivationFunctionType
ALU = mybir.AluOpType
AX_X = mybir.AxisListType.X

D = 1024
KT = D // P
T = 256
TT = T // P
EPS = 1e-6
NEG = -1e30
SLOTS = 4
BLK = 1024

CONV_CH, CONV_W = 512, 31
CT = CONV_CH // P
FOX_H, FOX_D = 8, 64
MEM_H, MEM_D = 4, 128
FF_CHUNKS = 4 * D // P
META = 16
SSD_H, SSD_D, SSD_G = 24, 64, 4
HG = SSD_H // SSD_G
GW = HG * SSD_D
D_SSD = SSD_H * SSD_D
XBC_T = (D_SSD + 2 * SSD_G * P) // P
XS_T = D_SSD // P
SC_T = 4
TM = META + T
PEER_H, TOPK, KEYS = 8, 16, 128
HK = PEER_H * TOPK
HALF = KEYS // 2
WIN = 32
BATCH = T // WIN
EXP_AT = (24, 52)

STREAM = {}
N_BLOCKS = 0
for _name, _n in (("ag", 8), ("qk", 8), ("v", 4), ("mk", 4), ("mv", 4), ("wout", 8), ("mq", 4), ("mo", 4),
                  ("mlp", 2 * FF_CHUNKS), ("xbc", XBC_T), ("sc", 3 * SC_T), ("z", 12), ("wout2", 16),
                  ("wq", 16), ("peer", 2 * KEYS)):
    STREAM[_name] = N_BLOCKS
    N_BLOCKS += _n

GAINS = 6
COL = {}
N_COLS = 0
for _name, _n in (("conv_w", CT * CONV_W), ("conv_b", CT), ("ln_g", CT), ("ln_b", CT), ("ssd_w", XBC_T * 4),
                  ("ssd_b", XBC_T), ("sc_w", SC_T * 3), ("w_f", KT * FOX_H), ("w_dt", KT * SSD_H)):
    COL[_name] = N_COLS
    N_COLS += _n
ROW = {}
N_ROWS = 0
for _name, _n in (("b_forget", FOX_H), ("dt_bias", SSD_H), ("a_log", SSD_H), ("d_skip", SSD_H),
                  ("ssd_norm", D_SSD)):
    ROW[_name] = N_ROWS
    N_ROWS += _n


LN_AT = (8, 11, 14)
TURN_AT = (0, 0, 1, 2, 3, 4)
SC_SPLIT_AT = (3, 5, 8, 11)


def turned_tiles():
    return [(c, META if c == 0 else P, 0 if c == 0 else META + P * (c - 1), q)
            for c in range(3) for q in range(4 if c < 2 else 3)]


class Steps:

    def __init__(self, eng, sem):
        self.eng, self.sem, self.n = eng, sem, 0

    def __call__(self, ins):
        ins.then_inc(self.sem, 1)
        self.n += 1
        return self.n

    def wait(self, n=None):
        self.eng.wait_ge(self.sem, self.n if n is None else n)


def build(nc, stream, gain_cols, cols, rows, post_gains, x, mem, meta, keys_in, out, h2_spill):
    ctx = ExitStack()
    with ctx:
        def sb(name, shape, dt=F32):
            return ctx.enter_context(nc.sbuf_tensor(name, shape, dt))

        def ps(name, shape):
            return ctx.enter_context(nc.psum_tensor(name, shape, F32))

        def sem(name):
            return ctx.enter_context(nc.semaphore(name))

        raw = sb("raw", [P, SLOTS, BLK])
        wh = sb("wh", [P, SLOTS, BLK], F32R)
        wl = sb("wl", [P, SLOTS, BLK], F32R)
        x_at = (nc.sbuf_base + 31) // 32 * 32
        X = sb("X", [P, TT, D])
        xh_at = (nc.sbuf_base + 31) // 32 * 32
        xh = sb("xh", [P, KT, TM], F32R)
        xl = sb("xl", [P, KT, TM], F32R)
        ident = sb("ident", [P, P])
        masks_at = (nc.sbuf_base + 31) // 32 * 32
        upper = sb("upper", [P, P])
        later = sb("later", [P, P])
        ones = sb("ones", [P, P])
        neg_half = sb("neg_half", [P, 1])
        ranks = sb("ranks", [P, TOPK])
        gain = sb("gain", [P, GAINS * KT])
        stat = sb("stat", [P, 48])
        choice_at = (nc.sbuf_base + 31) // 32 * 32
        i1T = sb("i1T", [P, T], BF16)
        i2T = sb("i2T", [P, T], BF16)
        gT = sb("gT", [P, 3, T], BF16)
        hot1 = sb("hot1", [P, 2, WIN, BATCH], BF16)
        arena_at = (nc.sbuf_base + 31) // 32 * 32
        arena = sb("arena", [P, 32 * BLK])

        def at(name, shape, offset, dt=F32, base=None):
            return nc.alloc_sbuf_tensor_at(name, shape, dt, offset=(arena_at if base is None else base) + offset)

        colp = at("colp", [P, N_COLS], 0)
        rowp = at("rowp", [P, N_ROWS], 2304)
        rowg = at("rowg", [P, 3, D], 8768)
        mask = at("mask", [P, 2 * P], 21056)
        memx = at("memx", [P, TT, D], 22080)
        AG = at("AG", [P, 2 * CT, T], 30272)
        QK = at("QK", [P, 8, T], 38464)
        V = at("V", [P, TT, 512], 46656)
        UP = at("UP", [P, CT, CONV_W - 1 + T], 50752)
        CV = at("CV", [P, CT, T], 55328)
        SQ = at("SQ", [P, CT, T], 59424)
        xn = at("xn", [P, 3, D], 63520)
        mh = at("mh", [P, KT, T], 79904, F32R)
        ml = at("ml", [P, KT, T], 88096, F32R)
        MK = at("MK", [P, 4, T], 96288)
        MV = at("MV", [P, TT, 512], 100384)
        DEC = at("DEC", [P, FOX_H, 3, P], 104480)
        att_s = at("att_s", [P, 2, 2 * P], 116768)
        att_p = at("att_p", [P, 2, 2 * P], 118816)
        att_pt = at("att_pt", [P, 2, 2, P], 120864)
        mixh = at("mixh", [P, 8, T], 22080, F32R)
        mixl = at("mixl", [P, 8, T], 30272, F32R)
        moh = at("moh", [P, 4, T], 38464, F32R)
        mol = at("mol", [P, 4, T], 42560, F32R)
        MQ = at("MQ", [P, 4, T], 46656)
        mlp_hid = at("mlp_hid", [P, 2, T], 50752)
        mlp_act = at("mlp_act", [P, 2, T], 52800)
        mlp_ah = at("mlp_ah", [P, 2, T], 54848, F32R)
        mlp_al = at("mlp_al", [P, 2, T], 56896, F32R)
        metax = at("metax", [META, D], 124192)
        SCX = at("SCX", [P, 3 * SC_T, TM], 8768)
        SP = at("SP", [P, SC_T, 2 + TM], 21824)
        sct = at("sct", [P, 2, T], 26240)
        SP_tmp = at("SP_tmp", [P, T], 124192)
        Z = at("Z", [P, TT, D_SSD], 28288)
        m2h = at("m2h", [P, 16, T], 40576, F32R)
        m2l = at("m2l", [P, 16, T], 56960, F32R)
        XB = at("XB", [P, XBC_T, 3 + TM], 79904)
        XS = at("XS", [P, XBC_T, TM], 102432)
        XT = at("XT", [P, 3, D_SSD], 79904)
        BN = at("BN", [P, 2, 4 * P], 98336)
        XDT = at("XDT", [P, TT, D_SSD], 8768)
        XDD = at("XDD", [P, D_SSD], 21056)
        ST = at("ST", [P, D_SSD], 0, base=xh_at)
        YO = (at("YO0", [P, D_SSD], 6144, base=xh_at), XDD)
        CBM = at("CBM", [P, 4, P], 12288, base=xh_at)
        AU = at("AU", [P, 2, 3, P], 124192)
        EE = at("EE", [P, 2, 3, P], 127264)
        MM = at("MM", [P, 2, 3, P], 73344)
        dtz = at("dtz", [P, 4, 72], 76416)
        exs = at("exs", [P, 120], 77568)
        QP = at("QP", [P, 16, T], 8768)
        hid = at("hid", [P, HALF, T], 0)
        gates = at("gates", [P, 2, WIN, T], 65536)
        keys = at("keys", [P, 16, KEYS], 122880)
        SCO = at("SCO", [P, TT, 16, KEYS], 73728)
        cand = at("cand", [P, PEER_H, TOPK * TOPK], 90112)
        eqs = at("eqs", [P, HK, TOPK], 98304)
        V16 = at("V16", [P, 16, TOPK], 106496)
        I16 = at("I16", [P, 16, TOPK], 107520, U32)
        I16F = at("I16F", [P, 16, TOPK], 108544)
        BV = at("BV", [P, TT, PEER_H, TOPK], 109568)
        BR = at("BR", [P, PEER_H, TOPK], 110592)
        PU = at("PU", [P, PEER_H, TOPK], 111104, U32)
        PA = at("PA", [P, 2, HK], 111616, U32)
        PF = at("PF", [P, 2, HK], 112640)
        NAT = at("NAT", [P, TT, 3, HK], 113664)
        gsum = at("gsum", [P, 2 * PEER_H], 116736)
        grest = at("grest", [P, 2, HK], 116800)
        hotA2 = at("hotA2", [P, KEYS, BATCH], 120832, BF16)
        hotB2 = at("hotB2", [P, 3, WIN, BATCH], 122880, BF16)
        peer_ah = at("peer_ah", [P, 2, T], 0, F32R, base=x_at)
        peer_al = at("peer_al", [P, 2, T], 2048, F32R, base=x_at)
        hotA = at("hotA", [P, KEYS, BATCH], 4096, BF16, base=x_at)
        numbers = at("numbers", [P, KEYS, BATCH], 6144, BF16, base=x_at)
        hotB = at("hotB", [P, 3, WIN, BATCH], 0, BF16, base=masks_at)
        fin_x = at("fin_x", [P, TT, D], 0)
        fin_g = at("fin_g", [P, D], 8192)
        fin_t = at("fin_t", [P, TT, D], 12288)
        fin_j = at("fin_j", [P, TT, D], 20480)

        Y = ps("Y", [P, TT, D])
        AO = ps("AO", [P, 2, 512])
        M = ps("M", [P, 2, 512])

        THIN = KT * (FOX_H + SSD_H)
        thin_h = at("thin_h", [P, THIN], 0, F32R, base=choice_at)
        thin_l = at("thin_l", [P, THIN], 4 * THIN, F32R, base=choice_at)

        landed = [sem(f"landed{s}") for s in range(SLOTS)]
        split_hi, split_lo = sem("split_hi"), sem("split_lo")
        w_used = sem("w_used")
        a_free = sem("a_free")
        x_in, mem_in, par_in, row_in = sem("x_in"), sem("mem_in"), sem("par_in"), sem("row_in")
        meta_in, keys_land = sem("meta_in"), sem("keys_land")
        consts = sem("consts")
        thin_hi, thin_lo = sem("thin_hi"), sem("thin_lo")
        vec_step, act_step, pool_step = sem("vec_step"), sem("act_step"), sem("pool_step")
        norm_ss, norm_rstd, norm_scaled = sem("norm_ss"), sem("norm_rstd"), sem("norm_scaled")
        norm_turned, norm_hi, norm_lo = sem("norm_turned"), sem("norm_hi"), sem("norm_lo")
        v_out, f_prod, mv_out = sem("v_out"), sem("f_prod"), sem("mv_out")
        gate_sig, conv_pad = sem("gate_sig"), sem("conv_pad")
        conv_step, conv_done = sem("conv_step"), sem("conv_done")
        f_z, f_ln, logf, dec_done = sem("f_z"), sem("f_ln"), sem("logf"), sem("dec_done")
        ln_sum, ln_xc, ln_sq, ln_y, ln_silu, ln_hi, ln_lo = (sem(n) for n in (
            "ln_sum", "ln_xc", "ln_sq", "ln_y", "ln_silu", "ln_hi", "ln_lo"))
        at_logit, at_max, at_neg, at_exp, at_inv, at_p = (sem(n) for n in (
            "at_logit", "at_max", "at_neg", "at_exp", "at_inv", "at_p"))
        at_turn, at_pt, at_pv, at_hi, at_lo = (sem(n) for n in ("at_turn", "at_pt", "at_pv", "at_hi", "at_lo"))
        post_ss, post_rstd, post_y, x_ready = sem("post_ss"), sem("post_rstd"), sem("post_y"), sem("x_ready")
        hid_prod, hid_hi, hid_lo = sem("hid_prod"), sem("hid_hi"), sem("hid_lo")
        xconv, xsilu, z_out = sem("xconv"), sem("xsilu"), sem("z_out")
        dt_prod, dt_z, dt_ln, dt_a = sem("dt_prod"), sem("dt_z"), sem("dt_ln"), sem("dt_a")
        sc_y, sc_hi, sc_lo = sem("sc_y"), sem("sc_hi"), sem("sc_lo")
        tr_in, tr_out = sem("tr_in"), sem("tr_out")
        cb_prod, cb_mask, ac_prod, ac_exp = sem("cb_prod"), sem("cb_mask"), sem("ac_prod"), sem("ac_exp")
        xdd_w, xdd_done, xdt_done, xd_done = sem("xdd_w"), sem("xdd_done"), sem("xdt_done"), sem("xd_done")
        st_prod, st_done = sem("st_prod"), sem("st_done")
        au_done, seg_prod, seg_exp, seg_m, y_prod = (sem(n) for n in (
            "au_done", "seg_prod", "seg_exp", "seg_m", "y_prod"))
        off_prod, off_done, y_add, y_gate = sem("off_prod"), sem("off_done"), sem("y_add"), sem("y_gate")
        grp_ss, grp_rstd, grp_y, y_turn, y_hi, y_lo = (sem(n) for n in (
            "grp_ss", "grp_rstd", "grp_y", "y_turn", "y_hi", "y_lo"))
        spilled, s_prod, s_out = sem("spilled"), sem("s_prod"), sem("s_out")
        top_sub, top_exp, top_nat, top_turn, top_T = (sem(n) for n in (
            "top_sub", "top_exp", "top_nat", "top_turn", "top_T"))
        numbered, hot_b, g_prod, g_out = sem("numbered"), sem("hot_b"), sem("g_prod"), sem("g_out")
        ln_var, ln_rstd, fin_rstd = sem("ln_var"), sem("ln_rstd"), sem("fin_rstd")
        fin_in, fin_ss, fin_y, stored = sem("fin_in"), sem("fin_ss"), sem("fin_y"), sem("stored")

        LAST = {k: STREAM[k] + n for k, n in (("qk", 8), ("ag", 8), ("v", 4), ("mk", 4), ("mv", 4), ("wout", 8),
                                              ("mq", 4), ("mo", 4), ("mlp", 2 * FF_CHUNKS), ("xbc", XBC_T),
                                              ("sc", 12), ("z", 12), ("wout2", 16), ("wq", 16),
                                              ("peer", 2 * KEYS))}
        A_BASE = {}
        n_a = 0
        for name, n in (("ag", 8), ("qk", 8), ("mk", 4), ("mq", 4), ("mlp", FF_CHUNKS), ("xbc", XBC_T),
                        ("sc", 12), ("wq", 16), ("peer", KEYS)):
            A_BASE[name] = n_a
            n_a += n

        def up_block(b0, c):
            return b0 if c == 0 else b0 + 2 * c - 1

        P0 = STREAM["peer"]

        def down_block(b0, c, n):
            return b0 + 2 * c + 2 if c < n - 1 else b0 + 2 * n - 1

        def pieces(n):
            two = [(X[:, j, :], P, j * P) for j in range(TT)]
            if n == 1:
                return [(memx[:, j, :], P, j * P) for j in range(TT)], mh, ml
            if n == 0 or n in (2, 3, 5):
                return two, xh, xl
            return [(s, r, META + c) for s, r, c in two] + [(metax[:, :], META, 0)], xh, xl

        NORM_TILES = [2, 2, 2, 2, 3, 2]

        units = [("fox", h, j) for h in range(FOX_H) for j in range(TT)]
        fox_units = len(units)
        units += [("mem", h, j) for h in range(MEM_H) for j in range(TT)]

        def unit_keys(u):
            kind, _, j = units[u]
            return P * (j + 1) if kind == "fox" else T

        def unit_dest(u):
            kind, h, j = units[u]
            if kind == "fox":
                r = FOX_D * (h % 2)
                return slice(r, r + FOX_D), mixh[:, CT + h // 2, P * j:P * j + P], mixl[:, CT + h // 2, P * j:P * j + P]
            return slice(0, P), moh[:, h, P * j:P * j + P], mol[:, h, P * j:P * j + P]

        block = ctx.enter_context(nc.Block())

        @block.sync
        def _(sp):
            sp.dma_start(X[:, :, :], x).then_inc(x_in, 16)
            for s in range(SLOTS):
                sp.dma_start(raw[:, s, :], stream[s]).then_inc(landed[s], 16)
            with sp.Fori(1, N_BLOCKS // SLOTS) as i:
                for s in range(SLOTS):
                    sp.wait_ge(split_lo, i * SLOTS + s - 3)
                    sp.dma_start(raw[:, s, :], stream[i * SLOTS + s]).then_inc(landed[s], 16)

        @block.scalar
        def _(act):
            step = Steps(act, act_step)
            act.dma_start(gain[:, :], gain_cols).then_inc(par_in, 16)
            act.dma_start(colp[:, :], cols).then_inc(par_in, 16)
            act.dma_start(rowp[:, :], rows.partition_broadcast(P)).then_inc(row_in, 16)
            act.dma_start(memx[:, :, :], mem).then_inc(mem_in, 16)
            for n in range(3):
                act.dma_start(rowg[:, n, :], post_gains[n].partition_broadcast(P)).then_inc(row_in, 16)
            act.dma_start(metax[:, :], meta).then_inc(meta_in, 16)

            def split(b0, j, i=0):
                b = b0 + j
                s = b % SLOTS
                act.wait_ge(landed[s], (i + b // SLOTS + 1) * 16)
                if not (type(i) is int and 4 * i + b < 4):
                    act.wait_ge(w_used, i * 4 + (b - 3))
                nc.scalar.copy(wh[:, s, :], raw[:, s, :]).then_inc(split_hi, 1)

            def split_ahead(b0, n):
                for j in range(n):
                    split(b0 + 4, j)

            def norm_scale(n, ready=None):
                tiles, _, _ = pieces(n)
                t0 = sum(NORM_TILES[:n])
                for k, (src, r, c) in enumerate(tiles):
                    if ready:
                        ready(k)
                    nc.scalar.activation(xn[0:r, k, :], src, ACT.Square,
                                         accum_out=stat[0:r, k:k + 1]).then_inc(norm_ss, 1)
                for k, (src, r, c) in enumerate(tiles):
                    act.wait_ge(norm_rstd, t0 + k + 1)
                    nc.scalar.activation(xn[0:r, k, :], src, ACT.Copy, scale=stat[0:r, 8 + k:9 + k])\
                        .then_inc(norm_scaled, 1)

            def norm_part(n, k, q):
                tiles, dh, _ = pieces(n)
                _, r, c = tiles[k]
                g = 2 * (sum(NORM_TILES[:n]) + k) + q
                act.wait_ge(norm_turned, g + 1)
                for i in range(4):
                    kt = 4 * q + i
                    ins = nc.scalar.activation(dh[:, kt, c:c + r], M[:, g % 2, P * i:P * i + r], ACT.Copy,
                                               scale=gain[:, n * KT + kt:n * KT + kt + 1])
                ins.then_inc(norm_hi, 1)

            def norm(n, ready=None):
                norm_scale(n, ready)
                for k in range(NORM_TILES[n]):
                    for q in range(2):
                        norm_part(n, k, q)

            def evac(name, j, dest, n=T, scale=1.0, i=0, func=ACT.Copy):
                e = A_BASE[name] + j
                act.wait_ge(w_used, i * 4 + (STREAM[name] + j + 1))
                nc.scalar.activation(dest, AO[:, e % 2, 0:n], func, scale=scale).then_inc(a_free, 1)

            norm_scale(0, lambda k: act.wait_ge(x_in, 16) if k == 0 else None)
            for j in range(SLOTS):
                split(0, j)
                if j == 1:
                    act.wait_ge(par_in, 32)
                    norm_part(0, 0, 0)
            for k, q in ((0, 1), (1, 0), (1, 1)):
                norm_part(0, k, q)
            nc.scalar.copy(thin_h[:, :], colp[:, COL["w_f"]:COL["w_f"] + THIN]).then_inc(thin_hi, 1)
            for j in range(8):
                evac("ag", j, AG[:, j, :])
                split(STREAM["ag"] + 4, j)
            step.eng.wait_ge(a_free, 8)
            nc.scalar.activation(AG[:, CT:, :], AG[:, CT:, :], ACT.Sigmoid).then_inc(gate_sig, 1)
            norm_scale(1, lambda k: act.wait_ge(mem_in, 16) if k == 0 else None)
            for j in range(8):
                evac("qk", j, QK[:, j, :], scale=FOX_D ** -0.5 if j < 4 else 1.0)
                split(STREAM["qk"] + 4, j)
                if 2 <= j < 6:
                    norm_part(1, (j - 2) // 2, j % 2)
            split_ahead(STREAM["v"], 4)
            act.wait_ge(w_used, LAST["v"])
            nc.scalar.copy(V[:, :, :], Y[:, 0, :].rearrange("p (j c) -> p j c", j=TT)).then_inc(v_out, 1)
            act.wait_ge(f_z, 2)
            step(nc.scalar.activation(stat[:, 32:48], stat[:, 32:48], ACT.Exp))
            step.wait()
            nc.scalar.activation(stat[:, 32:48], stat[:, 32:48], ACT.Ln, bias=1.0).then_inc(f_ln, 1)
            for j in range(4):
                evac("mk", j, MK[:, j, :])
                split(STREAM["mk"] + 4, j)
            split_ahead(STREAM["mv"], 4)
            act.wait_ge(w_used, LAST["mv"])
            nc.scalar.copy(MV[:, :, :], Y[:, 1, :].rearrange("p (j c) -> p j c", j=TT)).then_inc(mv_out, 1)
            def layer_norm(s):
                if s == LN_AT[0]:
                    act.wait_ge(dec_done, 3)
                    act.wait_ge(ln_xc, 1)
                    nc.scalar.activation(SQ[:, :, :], CV[:, :, :], ACT.Square).then_inc(ln_sq, 1)
                if s == LN_AT[1]:
                    act.wait_ge(ln_var, 1)
                    nc.scalar.activation(UP[:, 0, 0:T], UP[:, 0, 0:T], ACT.Sqrt).then_inc(ln_rstd, 1)
                if s == LN_AT[2]:
                    act.wait_ge(ln_y, 1)
                    for c in range(CT):
                        ins = nc.scalar.activation(SQ[:, c, :], CV[:, c, :], ACT.Silu,
                                                   bias=colp[:, COL["ln_b"] + c:COL["ln_b"] + c + 1],
                                                   scale=colp[:, COL["ln_g"] + c:COL["ln_g"] + c + 1])
                    ins.then_inc(ln_silu, 1)
                    act.wait_ge(ln_silu, 1)
                    nc.scalar.copy(mixh[:, 0:CT, :], SQ[:, :, :]).then_inc(ln_hi, 1)

            def attention(first, last, between=None):
                for s in range(first, last + 3):
                    if between:
                        between(s)
                    u = s
                    if u < last:
                        act.wait_ge(at_neg, u + 1)
                        if u >= 2:
                            act.wait_ge(at_turn, u - 1)
                        nk = unit_keys(u)
                        nc.scalar.activation(att_p[:, u % 2, 0:nk], att_s[:, u % 2, 0:nk], ACT.Exp,
                                             bias=stat[:, 18 + u % 2:19 + u % 2],
                                             accum_out=stat[:, 20 + u % 2:21 + u % 2]).then_inc(at_exp, 1)
                    u = s - 2
                    if first <= u < last:
                        act.wait_ge(at_turn, u + 1)
                        if u >= 2:
                            act.wait_ge(at_pv, u - 1)
                        n = unit_keys(u)
                        nc.scalar.copy(att_pt[:, u % 2, :, :].rearrange("p a b -> p (a b)")[:, 0:n],
                                       Y[:, 0, 512 * (u % 2):512 * (u % 2) + n]).then_inc(at_pt, 1)
                    u = s - 3
                    if first <= u < last:
                        rows_, dh, _ = unit_dest(u)
                        act.wait_ge(at_pv, u + 1)
                        nc.scalar.copy(dh[rows_, :], Y[rows_, 1, 512 * (u % 2):512 * (u % 2) + P])\
                            .then_inc(at_hi, 1)

            attention(0, fox_units, layer_norm)

            def post(p):
                for j in range(TT):
                    nc.scalar.activation(xn[:, j, :], Y[:, j, :], ACT.Square,
                                         accum_out=stat[:, 4 + j:5 + j]).then_inc(post_ss, 1)

            split_ahead(STREAM["wout"], 8)
            act.wait_ge(w_used, LAST["wout"])
            post(0)
            norm(2, lambda k: act.wait_ge(x_ready, k + 1))
            for j in range(4):
                evac("mq", j, MQ[:, j, :], scale=MEM_D ** -0.5)
                split(STREAM["mq"] + 4, j)
            attention(fox_units, len(units))
            split_ahead(STREAM["mo"], 4)
            act.wait_ge(w_used, LAST["mo"])
            post(1)
            norm(3, lambda k: act.wait_ge(x_ready, 2 + k + 1))

            def mlp(name, n, hid, act_, ah, func, base):
                b0 = STREAM[name]

                def hidden(s, i):
                    b = b0 if type(i) is int and i + s == 0 else b0 + 2 * s - 1
                    act.wait_ge(w_used, i * 4 + (b + 1))
                    nc.scalar.activation(hid[:, s, :], AO[:, s, 0:T], func).then_inc(a_free, 1)

                def high(s, i):
                    act.wait_ge(hid_prod, i * 2 + (base + s + 1))
                    nc.scalar.copy(ah[:, s, :], act_[:, s, :]).then_inc(hid_hi, 1)

                for s in range(2):
                    hidden(s, 0)
                    split(up_block(b0, s) + 4, 0)
                    high(s, 0)
                    if s:
                        split(down_block(b0, 0, n) + 4, 0)
                with act.Fori(1, n // 2 - 1) as i:
                    for s in range(2):
                        hidden(s, i)
                        split(b0 - 1 + 2 * s + 4, 0, i)
                        high(s, i)
                        split(b0 - 1 + 2 * s + 5, 0, i)
                i = n // 2 - 1
                for s in range(2):
                    c = 2 * i + s
                    hidden(s, i)
                    if up_block(b0, c) + 4 < N_BLOCKS:
                        split(up_block(b0, c) + 4, 0)
                    high(s, i)
                    if b0 + 2 * c + 4 < N_BLOCKS:
                        split(b0 + 2 * c + 4, 0)
                if b0 + 2 * n - 1 + 4 < N_BLOCKS:
                    split(b0 + 2 * n - 1 + 4, 0)

            mlp("mlp", FF_CHUNKS, mlp_hid, mlp_act, mlp_ah, ACT.Copy, 0)
            post(2)

            def ready4(k):
                if k == TT:
                    act.wait_ge(meta_in, 16)
                else:
                    act.wait_ge(x_ready, 4 + k + 1)
            norm(4, ready4)
            act.wait_ge(dt_z, 2)
            step(nc.scalar.activation(dtz[0:META, 1, 0:24], dtz[0:META, 1, 0:24], ACT.Exp))
            step(nc.scalar.activation(dtz[:, 1, 24:72], dtz[:, 1, 24:72], ACT.Exp))
            step(nc.scalar.activation(rowp[:, ROW["a_log"]:ROW["a_log"] + SSD_H],
                                      rowp[:, ROW["a_log"]:ROW["a_log"] + SSD_H], ACT.Exp))
            step.wait()
            nc.scalar.activation(dtz[0:META, 1, 0:24], dtz[0:META, 1, 0:24], ACT.Ln, bias=1.0).then_inc(dt_ln, 1)
            nc.scalar.activation(dtz[:, 1, 24:72], dtz[:, 1, 24:72], ACT.Ln, bias=1.0).then_inc(dt_ln, 1)
            for j in range(4):
                evac("xbc", j, XB[:, j, 3:], TM)
                split(STREAM["xbc"] + 4, j)
            with act.Fori(1, XBC_T // 4) as i:
                for j in range(4):
                    evac("xbc", j, XB[:, i * 4 + j, 3:], TM, i=i)
                    split(STREAM["xbc"] + 4, j, i)
                act.wait_ge(xconv, i * 16)
                nc.scalar.activation(XS[:, bass.ds(i * 4 - 4, 4), :], XS[:, bass.ds(i * 4 - 4, 4), :], ACT.Silu)\
                    .then_inc(xsilu, 1)
            act.wait_ge(xconv, 4 * XBC_T)
            nc.scalar.activation(XS[:, XBC_T - 4:, :], XS[:, XBC_T - 4:, :], ACT.Silu).then_inc(xsilu, 1)
            with act.Fori(0, SC_T * 3 // 4) as i:
                for j in range(4):
                    evac("sc", j, SCX[:, i * 4 + j, :], TM, i=i)
                    split(STREAM["sc"] + 4, j, i)
            turned = turned_tiles()

            def turned_out(n):
                c, r, _, q = turned[n]
                act.wait_ge(tr_in, n + 1)
                dst = XT[0:r, c, 512 * q:512 * q + 512] if q < 3 else BN[0:r, c, :]
                nc.scalar.copy(dst, M[0:r, n % 2, :]).then_inc(tr_out, 1)

            def sc_high(k):
                act.wait_ge(sc_y, k + 1)
                nc.scalar.copy(m2h[:, XS_T + k, :], sct[:, k % 2, :]).then_inc(sc_hi, 1)

            for j in range(12):
                split(STREAM["z"] + 4, j)
                if j < len(turned):
                    turned_out(j)
                if j in SC_SPLIT_AT:
                    sc_high(SC_SPLIT_AT.index(j))
                if j % 4 < 3:
                    continue
                g = j // 4
                act.wait_ge(w_used, STREAM["z"] + 4 * g + 4)
                nc.scalar.activation(Z[:, :, 512 * g:512 * g + 512],
                                     Y[:, g % 2, :].rearrange("p (j c) -> p j c", j=TT), ACT.Silu).then_inc(z_out, 1)
            act.wait_ge(ac_prod, 1)
            nc.scalar.activation(exs[:, 0:96], AO[:, 1, 0:96], ACT.Exp).then_inc(ac_exp, 1)
            nc.scalar.activation(exs[0:META, 96:120], AO[0:META, 1, 96:120], ACT.Exp).then_inc(ac_exp, 1)
            def squares(c):
                for g in range(SSD_G):
                    act.wait_ge(y_gate, c + 1)
                    nc.scalar.activation(XT[:, c + 1, GW * g:GW * g + GW], YO[c][:, GW * g:GW * g + GW], ACT.Square,
                                         accum_out=stat[:, 24 + g:25 + g]).then_inc(grp_ss, 1)

            for c in range(TT):
                for s in range(8):
                    if c and s == 2:
                        squares(0)
                    k = 8 * c + s
                    act.wait_ge(seg_prod, k + 1)
                    if k >= 2:
                        act.wait_ge(seg_m, k - 1)
                    nc.scalar.activation(EE[:, k % 2, :, :].rearrange("p a b -> p (a b)"), AO[:, k % 2, 0:3 * P],
                                         ACT.Exp).then_inc(seg_exp, 1)
            squares(1)
            for j in range(16):
                split(STREAM["wout2"] + 4, j)
                for k in range(6):
                    if TURN_AT[k] == j:
                        c, q = divmod(k, 3)
                        act.wait_ge(y_turn, k + 1)
                        nc.scalar.copy(m2h[:, 4 * q:4 * q + 4, P * c:P * c + P],
                                       M[:, k % 2, :].rearrange("p (k t) -> p k t", k=4)).then_inc(y_hi, 1)
            norm(5, lambda k: act.wait_ge(x_ready, 6 + k + 1))
            with act.Fori(0, 4) as i:
                for j in range(4):
                    evac("wq", j, QP[:, i * 4 + j, :], i=i)
                    split(STREAM["wq"] + 4, j, i)
            for q in range(8):
                act.wait_ge(s_prod, q + 1)
                nc.scalar.copy(SCO[:, q // 4, 4 * (q % 4):4 * (q % 4) + 4, :].rearrange("p a b -> p (a b)"),
                               Y[:, (q // 2) % 2, 512 * (q % 2):512 * (q % 2) + 512]).then_inc(s_out, 1)
            def hidden(c, b, s, i=0):
                act.wait_ge(w_used, i * 4 + (b + 1))
                nc.scalar.activation(hid[:, c, :], AO[:, s % 2, 0:T], ACT.Gelu).then_inc(a_free, 1)

            at_chunk = 0
            for j, until in enumerate(EXP_AT + (HALF,)):
                with act.Fori(at_chunk // 4, until // 4) as i:
                    for s in range(4):
                        hidden(i * 4 + s, P0 + s, s, i)
                        split(P0 + 4, s, i)
                at_chunk = until
                if j < TT:
                    act.wait_ge(top_sub, j + 1)
                    nc.scalar.activation(BV[:, j, :, :], BV[:, j, :, :], ACT.Exp).then_inc(top_exp, 1)
            for j in range(TT):
                act.wait_ge(top_turn, j + 1)
                for n, d in enumerate((i1T, i2T, gT[:, 0, :])):
                    ins = nc.scalar.copy(d[:, P * j:P * j + P], M[:, j, P * n:P * n + P])
                ins.then_inc(top_T, 1)

            def gates_out(window, base, c, bank):
                act.wait_ge(g_prod, c + (base + 1))
                nc.scalar.copy(gates[:, window % 2, :, bass.ds(c * BATCH, BATCH)],
                               M[:, bank, 0:WIN * BATCH].rearrange("p (t k) -> p k t", t=BATCH)).then_inc(g_out, 1)

            with act.Fori(0, WIN // 2) as i:
                for s in range(2):
                    gates_out(0, 0, i * 2 + s, s)

            def high_part(n, s, slot):
                act.wait_ge(hid_prod, n + (FF_CHUNKS + 1))
                nc.scalar.copy(peer_ah[:, s, :], hid[:, slot, :]).then_inc(hid_hi, 1)

            def both(c, s, i, first):
                high_part(c, s, c)
                if not first:
                    split(P0 + HALF + 3 + 2 * s, 0, i)
                act.wait_ge(hid_lo, c + (FF_CHUNKS + 1))
                split(P0 + HALF + 4 + 2 * s, 0, i)
                nc.scalar.activation(hid[:, c, :], AO[:, s, 0:T], ACT.Gelu).then_inc(a_free, 1)

            for w in range(2):
                if w == 0:
                    both(0, 0, 0, True)
                    gates_out(1, WIN, 0, 0)
                    both(1, 1, 0, False)
                    gates_out(1, WIN, 1, 1)
                with act.Fori(WIN // 2 * w + (w == 0), WIN // 2 * (w + 1)) as i:
                    for s in range(2):
                        both(i * 2 + s, s, i, False)
                        gates_out(w + 1, WIN * (w + 1), i * 2 + (s - WIN * w), s)
            def second(s, i, w):
                c = i * 4 + s
                if not (type(i) is int and c < 2):
                    act.wait_ge(w_used, c + (P0 + 3 * HALF - 1))
                high_part(c + HALF, s % 2, c)
                if not (type(i) is int and (c == 0 or c > HALF - 3)):
                    split(P0 + 3 * HALF + 2 + s, 0, i)
                if w == 2:
                    gates_out(3, 3 * WIN, c, s % 2)

            for i in (0, (1, WIN // 4), (WIN // 4, HALF // 4 - 1), HALF // 4 - 1):
                if type(i) is int:
                    for s in range(4):
                        second(s, i, 3 if i else 2)
                else:
                    with act.Fori(*i) as k:
                        for s in range(4):
                            second(s, k, 2 if i[0] == 1 else 3)
            act.wait_ge(w_used, N_BLOCKS)
            act.wait_ge(spilled, 16)
            act.dma_start(fin_x[:, :, :], h2_spill).then_inc(fin_in, 16)
            act.dma_start(fin_g[:, :], post_gains[3].partition_broadcast(P)).then_inc(fin_in, 16)
            for j in range(TT):
                act.wait_ge(fin_y, j + 1)
                nc.scalar.activation(fin_j[:, j, :], fin_t[:, j, :], ACT.Square,
                                     accum_out=stat[:, 4 + j:5 + j]).then_inc(fin_ss, 1)
            for j in range(TT):
                act.wait_ge(fin_y, 2 + j + 1)
                act.dma_start(out[:, j, :], fin_x[:, j, :]).then_inc(stored, 16)
            act.wait_ge(stored, 32)

        @block.vector
        def _(dve):
            step = Steps(dve, vec_step)

            def split(b0, j, i=0):
                b = b0 + j
                dve.wait_ge(split_hi, i * 4 + (b + 1))
                s = b % SLOTS
                nc.vector.tensor_tensor(wl[:, s, :], raw[:, s, :], wh[:, s, :].bitcast(F32), ALU.subtract)\
                    .then_inc(split_lo, 1)

            def split_ahead(b0, n):
                for j in range(n):
                    split(b0 + 4, j)

            def norm_part(n, k, q):
                tiles, dh, dl = pieces(n)
                _, r, c = tiles[k]
                g = 2 * (sum(NORM_TILES[:n]) + k) + q
                dve.wait_ge(norm_hi, g + 1)
                for i in range(4):
                    kt = 4 * q + i
                    ins = nc.vector.scalar_tensor_tensor(
                        out=dl[:, kt, c:c + r], in0=M[:, g % 2, P * i:P * i + r],
                        scalar=gain[:, n * KT + kt:n * KT + kt + 1],
                        in1=dh[:, kt, c:c + r].bitcast(F32), op0=ALU.mult, op1=ALU.subtract)
                ins.then_inc(norm_lo, 1)

            def norm(n):
                for k in range(NORM_TILES[n]):
                    for q in range(2):
                        norm_part(n, k, q)

            def col(name, k):
                return colp[:, COL[name] + k:COL[name] + k + 1]

            nc.vector.memset(UP[:, :, 0:CONV_W - 1], 0.0).then_inc(conv_pad, 1)
            for j in range(SLOTS):
                split(0, j)
            dve.wait_ge(par_in, 32)
            norm(0)
            dve.wait_ge(thin_hi, 1)
            nc.vector.tensor_tensor(thin_l[:, :], colp[:, COL["w_f"]:COL["w_f"] + THIN], thin_h[:, :].bitcast(F32),
                                    ALU.subtract).then_inc(thin_lo, 1)
            split_ahead(STREAM["ag"], 8)
            dve.wait_ge(gate_sig, 1)
            nc.vector.tensor_tensor(UP[:, :, CONV_W - 1:], AG[:, 0:CT, :], AG[:, CT:, :], ALU.mult)\
                .then_inc(conv_pad, 1)
            dve.wait_ge(conv_pad, 2)

            taps = [(w, c) for w in range(CONV_W) for c in range(CT)]

            def conv(k):
                w, c = taps[k]
                src = UP[:, c, w:w + T]
                if w == 0:
                    nc.vector.tensor_scalar(CV[:, c, :], src, col("conv_w", c * CONV_W), col("conv_b", c),
                                            ALU.mult, ALU.add).then_inc(conv_step, 1)
                else:
                    dve.wait_ge(conv_step, k - CT + 1)
                    nc.vector.scalar_tensor_tensor(out=CV[:, c, :], in0=src,
                                                   scalar=col("conv_w", c * CONV_W + w), in1=CV[:, c, :],
                                                   op0=ALU.mult, op1=ALU.add).then_inc(conv_step, 1)

            done = [0]

            def some_taps(n):
                for k in range(done[0], min(done[0] + n, len(taps))):
                    conv(k)
                done[0] = min(done[0] + n, len(taps))

            for j in range(8):
                split(STREAM["qk"] + 4, j)
                some_taps(3 if 2 <= j < 6 else 5)
                if 2 <= j < 6:
                    norm_part(1, (j - 2) // 2, j % 2)
            for j in range(4):
                split(STREAM["v"] + 4, j)
                some_taps(6)
            dve.wait_ge(f_prod, 1)
            dve.wait_ge(row_in, 64)
            z8 = stat[:, 32:48].rearrange("p (j h) -> p j h", j=TT)
            zf = SQ[:, 0, 0:16].rearrange("p (j h) -> p j h", j=TT)
            bf = rowp[:, ROW["b_forget"]:ROW["b_forget"] + FOX_H]
            step(nc.vector.tensor_tensor(zf, M[:, 0, 0:16].rearrange("p (j h) -> p j h", j=TT),
                                         bf[:, None, :].to_broadcast([P, TT, FOX_H]), ALU.add))
            step.wait()
            nc.vector.scalar_tensor_tensor(out=z8, in0=zf, scalar=-1.0, in1=zf, op0=ALU.mult, op1=ALU.min)\
                .then_inc(f_z, 1)
            nc.vector.tensor_scalar(zf, zf, 0.0, None, ALU.min).then_inc(f_z, 1)
            some_taps(6)
            dve.wait_ge(f_ln, 1)
            nc.vector.tensor_tensor(zf, zf, z8, ALU.subtract).then_inc(logf, 1)
            for j in range(4):
                split(STREAM["mk"] + 4, j)
                some_taps(4)
            for j in range(4):
                split(STREAM["mv"] + 4, j)
                some_taps(4)
            def layer_norm(s):
                v = UP[:, 0, 0:T]
                if s < LN_AT[0] - 1:
                    some_taps(4)
                if s == LN_AT[0] - 1:
                    some_taps(len(taps))
                    dve.wait_ge(conv_step, len(taps))
                    nc.vector.tensor_copy(stat[:, 14:15], CV[:, 0, 0:1]).then_inc(conv_done, 1)
                if s == LN_AT[0]:
                    dve.wait_ge(ln_sum, 1)
                    nc.vector.scalar_tensor_tensor(out=CV[:, :, :],
                                                   in0=AO[:, 0, 0:T][:, None, :].to_broadcast([P, CT, T]),
                                                   scalar=-1.0 / CONV_CH, in1=CV[:, :, :], op0=ALU.mult,
                                                   op1=ALU.add).then_inc(ln_xc, 1)
                if s == LN_AT[1]:
                    dve.wait_ge(ln_sum, 2)
                    nc.vector.tensor_scalar(v, AO[:, 1, 0:T], 1.0 / CONV_CH, EPS, ALU.mult, ALU.add).then_inc(ln_var, 1)
                if s == LN_AT[1] + 2:
                    dve.wait_ge(ln_rstd, 1)
                    step(nc.vector.reciprocal(v, v))
                    step.wait()
                    nc.vector.tensor_tensor(CV[:, :, :], CV[:, :, :], v[:, None, :].to_broadcast([P, CT, T]), ALU.mult)\
                        .then_inc(ln_y, 1)
                if s == LN_AT[2] + 3:
                    dve.wait_ge(ln_hi, 1)
                    nc.vector.tensor_tensor(mixl[:, 0:CT, :], SQ[:, :, :], mixh[:, 0:CT, :].bitcast(F32), ALU.subtract)\
                        .then_inc(ln_lo, 1)

            def attention(first, last, between=None):
                for s in range(first, last + 4):
                    if between:
                        between(s)
                    u = s
                    if u < last:
                        kind, _, j = units[u]
                        nk = unit_keys(u)
                        m = mask[:, P:2 * P] if (kind, j) == ("fox", 0) else mask[:, 0:2 * P] if kind == "fox" \
                            else None
                        dve.wait_ge(at_logit, u + 1)
                        if u >= 2:
                            dve.wait_ge(at_exp, u - 1)
                        if m is None:
                            step(nc.vector.tensor_copy(att_s[:, u % 2, 0:nk], M[:, u % 2, 0:nk]))
                            nc.vector.tensor_reduce(stat[:, 16 + u % 2:17 + u % 2], M[:, u % 2, 0:nk], AX_X,
                                                    ALU.max).then_inc(at_max, 1)
                        else:
                            nc.vector.tensor_tensor_reduce(att_s[:, u % 2, 0:nk], M[:, u % 2, 0:nk], m, 1.0, 3 * NEG,
                                                           ALU.add, ALU.max, stat[:, 16 + u % 2:17 + u % 2])\
                                .then_inc(at_max, 1)
                        dve.wait_ge(at_max, u + 1)
                        nc.vector.tensor_scalar(stat[:, 18 + u % 2:19 + u % 2], stat[:, 16 + u % 2:17 + u % 2],
                                                -1.0, None, ALU.mult).then_inc(at_neg, 1)
                    u = s - 1
                    if first <= u < last:
                        dve.wait_ge(at_exp, u + 1)
                        nc.vector.reciprocal(stat[:, 22 + u % 2:23 + u % 2], stat[:, 20 + u % 2:21 + u % 2])\
                            .then_inc(at_inv, 1)
                        dve.wait_ge(at_inv, u + 1)
                        nk = unit_keys(u)
                        nc.vector.tensor_scalar(att_p[:, u % 2, 0:nk], att_p[:, u % 2, 0:nk],
                                                stat[:, 22 + u % 2:23 + u % 2], None, ALU.mult).then_inc(at_p, 1)
                    u = s - 3
                    if first <= u < last:
                        rows_, dh, dl = unit_dest(u)
                        dve.wait_ge(at_hi, u + 1)
                        nc.vector.tensor_tensor(dl[rows_, :], Y[rows_, 1, 512 * (u % 2):512 * (u % 2) + P],
                                                dh[rows_, :].bitcast(F32), ALU.subtract).then_inc(at_lo, 1)

            def post(p):
                for j in range(TT):
                    dve.wait_ge(post_rstd, 2 * p + j + 1)
                    nc.vector.scalar_tensor_tensor(out=xn[:, j, :], in0=Y[:, j, :], scalar=stat[:, 12 + j:13 + j],
                                                   in1=rowg[:, p, :], op0=ALU.mult, op1=ALU.mult)\
                        .then_inc(post_y, 1)
                    dve.wait_ge(post_y, 2 * p + j + 1)
                    nc.vector.tensor_tensor(X[:, j, :], X[:, j, :], xn[:, j, :], ALU.add).then_inc(x_ready, 1)

            attention(0, fox_units, layer_norm)
            split_ahead(STREAM["wout"], 8)
            post(0)
            norm(2)
            split_ahead(STREAM["mq"], 4)
            attention(fox_units, len(units))
            split_ahead(STREAM["mo"], 4)
            post(1)
            norm(3)

            def squared_relu(hid, dst, c):
                return nc.vector.scalar_tensor_tensor(out=dst, in0=hid, scalar=0.0, in1=hid,
                                                      op0=ALU.max, op1=ALU.mult)

            def weighed(hid, dst, c):
                return nc.vector.tensor_tensor(dst, hid, gates[:, c, :], ALU.mult)

            def mlp(name, n, hid, act_, ah, al, func, free_base, base):
                b0 = STREAM[name]

                def hidden(c, s, i):
                    dve.wait_ge(a_free, i * 2 + (free_base + s + 1))
                    func(hid[:, s, :], act_[:, s, :], c).then_inc(hid_prod, 1)

                def low(s, i):
                    dve.wait_ge(hid_hi, i * 2 + (base + s + 1))
                    nc.vector.tensor_tensor(al[:, s, :], act_[:, s, :], ah[:, s, :].bitcast(F32), ALU.subtract)\
                        .then_inc(hid_lo, 1)

                for s in range(2):
                    hidden(s, s, 0)
                    split(up_block(b0, s) + 4, 0)
                    low(s, 0)
                    if s:
                        split(down_block(b0, 0, n) + 4, 0)
                with dve.Fori(1, n // 2 - 1) as i:
                    for s in range(2):
                        hidden(i * 2 + s, s, i)
                        split(b0 - 1 + 2 * s + 4, 0, i)
                        low(s, i)
                        split(b0 - 1 + 2 * s + 5, 0, i)
                for s in range(2):
                    i = n // 2 - 1
                    c = 2 * i + s
                    hidden(c, s, i)
                    if up_block(b0, c) + 4 < N_BLOCKS:
                        split(up_block(b0, c) + 4, 0)
                    low(s, i)
                    if down_block(b0, c - 1, n) + 4 < N_BLOCKS:
                        split(down_block(b0, c - 1, n) + 4, 0)
                if down_block(b0, n - 1, n) + 4 < N_BLOCKS:
                    split(down_block(b0, n - 1, n) + 4, 0)

            mlp("mlp", FF_CHUNKS, mlp_hid, mlp_act, mlp_ah, mlp_al, squared_relu, A_BASE["mlp"], 0)
            post(2)

            norm(4)
            step(nc.vector.memset(XB[:, :, 0:3], 0.0))
            dve.wait_ge(dt_prod, 1)
            db = rowp[:, ROW["dt_bias"]:ROW["dt_bias"] + SSD_H]
            ea = rowp[:, ROW["a_log"]:ROW["a_log"] + SSD_H]
            parts = ((META, 0, 1), (P, 24, 2))
            for r, o, n in parts:
                step(nc.vector.tensor_tensor(dtz[0:r, 0, o:o + 24 * n].rearrange("p (j h) -> p j h", j=n),
                                             M[0:r, 0, o:o + 24 * n].rearrange("p (j h) -> p j h", j=n),
                                             db[0:r, None, :].to_broadcast([r, n, SSD_H]), ALU.add))
            step.wait()
            for r, o, n in parts:
                z = dtz[0:r, 0, o:o + 24 * n]
                nc.vector.scalar_tensor_tensor(out=dtz[0:r, 1, o:o + 24 * n], in0=z, scalar=-1.0, in1=z,
                                               op0=ALU.mult, op1=ALU.min).then_inc(dt_z, 1)
            dve.wait_ge(dt_ln, 2)
            for r, o, n in parts:
                step(nc.vector.scalar_tensor_tensor(out=dtz[0:r, 2, o:o + 24 * n], in0=dtz[0:r, 0, o:o + 24 * n],
                                                    scalar=0.0, in1=dtz[0:r, 1, o:o + 24 * n],
                                                    op0=ALU.max, op1=ALU.add))
            step.wait()
            for r, o, n in parts:
                nc.vector.scalar_tensor_tensor(
                    out=dtz[0:r, 3, o:o + 24 * n].rearrange("p (j h) -> p j h", j=n),
                    in0=dtz[0:r, 2, o:o + 24 * n].rearrange("p (j h) -> p j h", j=n), scalar=-1.0,
                    in1=ea[0:r, None, :].to_broadcast([r, n, SSD_H]), op0=ALU.mult, op1=ALU.mult)\
                    .then_inc(dt_a, 1)

            def conv4(i):
                for w in range(4):
                    for j in range(4):
                        src = XB[:, i * 4 + j, w:w + TM]
                        dst = XS[:, i * 4 + j, :]
                        o = COL["ssd_w"]
                        wt = colp[:, bass.ds(i * 16 + (o + 4 * j + w), 1)]
                        if w == 0:
                            bias = colp[:, bass.ds(i * 4 + (COL["ssd_b"] + j), 1)]
                            nc.vector.tensor_scalar(dst, src, wt, bias, ALU.mult, ALU.add).then_inc(xconv, 1)
                        else:
                            dve.wait_ge(xconv, i * 16 + (4 * w + j - 3))
                            nc.vector.scalar_tensor_tensor(out=dst, in0=src, scalar=wt, in1=dst,
                                                           op0=ALU.mult, op1=ALU.add).then_inc(xconv, 1)

            with dve.Fori(0, XBC_T // 4) as i:
                for j in range(4):
                    split(STREAM["xbc"] + 4, j, i)
                dve.wait_ge(a_free, i * 4 + (A_BASE["xbc"] + 4))
                conv4(i)
            with dve.Fori(0, SC_T * 3 // 4) as i:
                for j in range(4):
                    split(STREAM["sc"] + 4, j, i)
            for j in range(12):
                split(STREAM["z"] + 4, j)
                if j in SC_SPLIT_AT:
                    k = SC_SPLIT_AT.index(j)
                    dve.wait_ge(sc_hi, k + 1)
                    nc.vector.tensor_tensor(m2l[:, XS_T + k, :], sct[:, k % 2, :], m2h[:, XS_T + k, :].bitcast(F32),
                                            ALU.subtract).then_inc(sc_lo, 1)
            dve.wait_ge(ac_exp, 2)
            nc.vector.tensor_tensor(exs[0:META, 96:120], exs[0:META, 96:120], dtz[0:META, 2, 0:24], ALU.mult)\
                .then_inc(xdd_w, 1)
            nc.vector.tensor_tensor(exs[:, 48:72], exs[:, 48:72], dtz[:, 2, 24:48], ALU.mult).then_inc(xdd_w, 1)

            def heads(t, o=0):
                return t[:, o:o + GW].rearrange("p (h d) -> p h d", h=HG)

            def per_head(col0, g, n=HG, w=SSD_D):
                return exs[:, col0 + HG * g:col0 + HG * g + n][:, :, None].to_broadcast([P, n, w])

            for g in range(SSD_G):
                dve.wait_ge(st_prod, g + 1)
                nc.vector.tensor_copy(ST[:, GW * g:GW * g + GW], M[:, g % 2, 0:GW]).then_inc(st_done, 1)
            def group_norm(c):
                dve.wait_ge(grp_rstd, c + 1)
                for g in range(SSD_G):
                    nc.vector.scalar_tensor_tensor(
                        out=YO[c][:, GW * g:GW * g + GW], in0=YO[c][:, GW * g:GW * g + GW],
                        scalar=stat[:, 28 + g:29 + g],
                        in1=rowp[:, ROW["ssd_norm"] + GW * g:ROW["ssd_norm"] + GW * g + GW],
                        op0=ALU.mult, op1=ALU.mult).then_inc(grp_y, 1)

            for c in range(TT):
                dve.wait_ge(cb_prod, c + 1)
                nc.vector.tensor_tensor(CBM[:, :, :], M[:, 0, :].rearrange("p (g l) -> p g l", g=SSD_G),
                                        upper[:, None, :].to_broadcast([P, SSD_G, P]), ALU.mult).then_inc(cb_mask, 1)
                dve.wait_ge(cb_mask, c + 1)
                for s in range(8):
                    k = 8 * c + s
                    if c and s == 6:
                        group_norm(0)
                    dve.wait_ge(seg_exp, k + 1)
                    if k >= 2:
                        dve.wait_ge(y_prod, k - 1)
                    nc.vector.tensor_tensor(MM[:, k % 2, :, :], EE[:, k % 2, :, :],
                                            CBM[:, s // 2, :][:, None, :].to_broadcast([P, 3, P]), ALU.mult)\
                        .then_inc(seg_m, 1)
                    if s % 2:
                        g = s // 2
                        dve.wait_ge(off_prod, 4 * c + g + 1)
                        nc.vector.tensor_tensor(heads(YO[c], GW * g), heads(M[:, (g + 1) % 2, :]),
                                                per_head(24 * c, g), ALU.mult).then_inc(off_done, 1)
                if c == 0:
                    for g in range(SSD_G):
                        dve.wait_ge(off_prod, 4)
                        step(nc.vector.tensor_tensor(heads(ST, GW * g), heads(ST, GW * g), per_head(72, g), ALU.mult))
                    step.wait()
                    for g in range(SSD_G):
                        dve.wait_ge(st_prod, SSD_G + g + 1)
                        nc.vector.tensor_tensor(ST[:, GW * g:GW * g + GW], ST[:, GW * g:GW * g + GW],
                                                M[:, g % 2, 0:GW], ALU.add).then_inc(st_done, 1)
                dve.wait_ge(y_prod, 8 * c + 8)
                dve.wait_ge(off_done, 4 * c + 4)
                yd = Y[:, :, :].rearrange("p a b -> p (a b)")[:, 0:D_SSD]
                nc.vector.tensor_tensor(YO[c][:, :], YO[c][:, :], yd, ALU.add).then_inc(y_add, 1)
                dve.wait_ge(y_add, 2 * c + 1)
                dve.wait_ge(xd_done, c + 1)
                nc.vector.tensor_tensor(YO[c][:, :], YO[c][:, :], XT[:, c + 1, :], ALU.add).then_inc(y_add, 1)
                dve.wait_ge(y_add, 2 * c + 2)
                dve.wait_ge(z_out, 3)
                nc.vector.tensor_tensor(YO[c][:, :], YO[c][:, :], Z[:, c, :], ALU.mult).then_inc(y_gate, 1)

            for j in range(16):
                if j == 1:
                    group_norm(1)
                split(STREAM["wout2"] + 4, j)
                for k in range(6):
                    if TURN_AT[k] == j:
                        c, q = divmod(k, 3)
                        dve.wait_ge(y_hi, k + 1)
                        nc.vector.tensor_tensor(m2l[:, 4 * q:4 * q + 4, P * c:P * c + P],
                                                M[:, k % 2, :].rearrange("p (k t) -> p k t", k=4),
                                                m2h[:, 4 * q:4 * q + 4, P * c:P * c + P].bitcast(F32),
                                                ALU.subtract).then_inc(y_lo, 1)
            for j in range(TT):
                dve.wait_ge(w_used, LAST["wout2"])
                nc.vector.tensor_tensor(X[:, j, :], X[:, j, :], Y[:, j, :], ALU.add).then_inc(x_ready, 1)
            norm(5)
            with dve.Fori(0, 4) as i:
                for j in range(4):
                    split(STREAM["wq"] + 4, j, i)

            turns = [0, 0]

            def turn(ins):
                step(ins)
                turns[0] += 1
                if turns[0] % 6 == 0 and turns[1] < HALF:
                    split(P0 + 4, turns[1])
                    turns[1] += 1

            def splits_until(n):
                while turns[1] < n:
                    split(P0 + 4, turns[1])
                    turns[1] += 1

            def best16(n, vals, top, pos):
                for half in (slice(0, 8), slice(8, 16)):
                    for k in range(n):
                        turn(nc.vector.max(top(k)[:, half], vals(k)))
                    step.wait()
                    for k in range(n):
                        turn(nc.vector.max_index(pos(k)[:, half], top(k)[:, half], vals(k)))
                    step.wait()
                    if half.start == 0:
                        for k in range(n):
                            turn(nc.vector.match_replace(vals(k), top(k)[:, half], vals(k), 3 * NEG))
                        step.wait()

            for j in range(TT):
                dve.wait_ge(s_out, 4 * j + 4)
                best16(16, lambda k: SCO[:, j, k, :], lambda k: V16[:, k, :], lambda k: I16[:, k, :])
                turn(nc.vector.tensor_copy(I16F[:, :, :], I16[:, :, :]))
                for h in range(PEER_H):
                    turn(nc.vector.tensor_tensor(
                        cand[:, h, :].rearrange("p (a b) -> p a b", a=TOPK),
                        V16[:, 2 * h, :][:, :, None].to_broadcast([P, TOPK, TOPK]),
                        V16[:, 2 * h + 1, :][:, None, :].to_broadcast([P, TOPK, TOPK]), ALU.add))
                step.wait()
                best16(8, lambda h: cand[:, h, :], lambda h: BR[:, h, :], lambda h: PU[:, h, :])
                splits_until(EXP_AT[j])
                nc.vector.tensor_tensor(BV[:, j, :, :], BR[:, :, :],
                                        BR[:, :, 0:1].to_broadcast([P, PEER_H, TOPK]), ALU.subtract)\
                    .then_inc(top_sub, 1)
                turn(nc.vector.tensor_scalar(PA[:, 0, :], PU[:, :, :].rearrange("p h k -> p (h k)"), 4, None,
                                             ALU.logical_shift_right))
                turn(nc.vector.tensor_scalar(PA[:, 1, :], PU[:, :, :].rearrange("p h k -> p (h k)"), 15, None,
                                             ALU.bitwise_and))
                step.wait()
                turn(nc.vector.tensor_copy(PF[:, :, :], PA[:, :, :]))
                for half in range(2):
                    step.wait()
                    for q in range(4):
                        e = slice(32 * q, 32 * q + 32)
                        turn(nc.vector.tensor_tensor(eqs[:, e, :],
                                                     PF[:, half, e][:, :, None].to_broadcast([P, 32, TOPK]),
                                                     ranks[:, None, :].to_broadcast([P, 32, TOPK]), ALU.is_equal))
                    step.wait()
                    for h in range(PEER_H):
                        e = eqs[:, TOPK * h:TOPK * h + TOPK, :]
                        turn(nc.vector.tensor_tensor(
                            e, e, I16F[:, 2 * h + half, :][:, None, :].to_broadcast([P, TOPK, TOPK]), ALU.mult))
                    step.wait()
                    for q in range(4):
                        e = slice(32 * q, 32 * q + 32)
                        turn(nc.vector.tensor_reduce(NAT[:, j, half, e], eqs[:, e, :], AX_X, ALU.add))
                dve.wait_ge(top_exp, j + 1)
                turn(nc.vector.tensor_reduce(gsum[:, 0:PEER_H], BV[:, j, :, :], AX_X, ALU.add))
                step.wait()
                turn(nc.vector.reciprocal(gsum[:, PEER_H:], gsum[:, 0:PEER_H]))
                step.wait()
                nc.vector.tensor_tensor(NAT[:, j, 2, :].rearrange("p (h k) -> p h k", h=PEER_H), BV[:, j, :, :],
                                        gsum[:, PEER_H:][:, :, None].to_broadcast([P, PEER_H, TOPK]), ALU.mult)\
                    .then_inc(top_nat, 1)
            splits_until(HALF)
            for j in range(TT):
                dve.wait_ge(top_T, j + 1)
                tok = slice(P * j, P * j + P)
                step(nc.vector.tensor_tensor(grest[:, 0, :], M[:, j, 2 * P:3 * P], gT[:, 0, tok], ALU.subtract))
                step.wait()
                step(nc.vector.tensor_copy(gT[:, 1, tok], grest[:, 0, :]))
                step.wait()
                step(nc.vector.tensor_tensor(gT[:, 2, tok], grest[:, 0, :], gT[:, 1, tok], ALU.subtract))
                step.wait()
            dve.wait_ge(numbered, 1)

            def hot(window, base, c, s, A, B, read=True):
                t = bass.ds(c * BATCH, BATCH)
                if read:
                    dve.wait_ge(hot_b, c * 5 + (5 * base - 5))
                nc.vector.tensor_tensor(hot1[:, s, :, :], numbers[:, WIN * window:WIN * window + WIN, :],
                                        i1T[:, t][:, None, :].to_broadcast([P, WIN, BATCH]), ALU.is_equal)\
                    .then_inc(hot_b, 1)
                nc.vector.tensor_tensor(A[:, :, :], numbers[:, :, :],
                                        i2T[:, t][:, None, :].to_broadcast([P, KEYS, BATCH]), ALU.is_equal)\
                    .then_inc(hot_b, 1)
                dve.wait_ge(hot_b, c * 5 + (5 * base + 1))
                for n in range(3):
                    nc.vector.tensor_tensor(B[:, n, :, :], hot1[:, s, :, :],
                                            gT[:, n, t][:, None, :].to_broadcast([P, WIN, BATCH]), ALU.mult)\
                        .then_inc(hot_b, 1)

            for s, (A, B) in enumerate(((hotA, hotB), (hotA2, hotB2))):
                hot(0, 0, s, s, A, B, False)
            with dve.Fori(1, WIN // 2) as i:
                for s, (A, B) in enumerate(((hotA, hotB), (hotA2, hotB2))):
                    dve.wait_ge(g_prod, i * 2 + (s - 1))
                    hot(0, 0, i * 2 + s, s, A, B)

            def weigh(slot, window, chunk):
                nc.vector.tensor_tensor(hid[:, slot, :], hid[:, slot, :], gates[:, window % 2, chunk, :], ALU.mult)\
                    .then_inc(hid_prod, 1)

            def low_part(n, s, slot):
                dve.wait_ge(hid_hi, n + (FF_CHUNKS + 1))
                nc.vector.tensor_tensor(peer_al[:, s, :], hid[:, slot, :], peer_ah[:, s, :].bitcast(F32),
                                        ALU.subtract).then_inc(hid_lo, 1)

            def next_gates(window, c, s):
                dve.wait_ge(g_prod, c + WIN * window)
                hot(window, WIN * window, c, s, hotA, hotB)

            def both(c, s, i, w, first):
                weigh(c, w, c + (-WIN * w))
                next_gates(w + 1, c + (-WIN * w), s)
                low_part(c, s, c)
                if not first:
                    split(P0 + HALF + 3 + 2 * s, 0, i)
                split(P0 + HALF + 4 + 2 * s, 0, i)

            dve.wait_ge(g_out, WIN)
            for w in range(2):
                if w:
                    dve.wait_ge(g_out, 2 * WIN)
                if w == 0:
                    both(0, 0, 0, w, True)
                    both(1, 1, 0, w, False)
                with dve.Fori(WIN // 2 * w + (w == 0), WIN // 2 * (w + 1)) as i:
                    for s in range(2):
                        both(i * 2 + s, s, i, w, False)
            def second(s, i, w):
                c = i * 4 + s
                weigh(c, w, c + (2 - w) * WIN)
                if w == 2:
                    next_gates(3, c, s % 2)
                if not (type(i) is int and (c < 2 or c == HALF - 1)):
                    split(P0 + 3 * HALF + 1 + s, 0, i)
                low_part(c + HALF, s % 2, c)

            for i in (0, (1, WIN // 4), (WIN // 4, HALF // 4 - 1), HALF // 4 - 1):
                if type(i) is int:
                    if i == 0:
                        dve.wait_ge(g_out, 3 * WIN)
                    for s in range(4):
                        second(s, i, 3 if i else 2)
                else:
                    if i[0] > 1:
                        dve.wait_ge(g_out, 4 * WIN)
                    with dve.Fori(*i) as k:
                        for s in range(4):
                            second(s, k, 2 if i[0] == 1 else 3)
            dve.wait_ge(w_used, N_BLOCKS)
            dve.wait_ge(fin_in, 32)
            for j in range(TT):
                nc.vector.tensor_tensor(fin_t[:, j, :], fin_x[:, j, :], Y[:, j, :], ALU.add).then_inc(fin_y, 1)
            for j in range(TT):
                dve.wait_ge(fin_rstd, j + 1)
                nc.vector.scalar_tensor_tensor(out=fin_x[:, j, :], in0=fin_t[:, j, :], scalar=stat[:, 12 + j:13 + j],
                                               in1=fin_g[:, :], op0=ALU.mult, op1=ALU.mult).then_inc(fin_y, 1)

        @block.gpsimd
        def _(pool):
            step = Steps(pool, pool_step)
            nc.gpsimd.memset(ones[:, :], 1.0).then_inc(consts, 1)
            nc.gpsimd.memset(ident[:, :], 0.0).then_inc(consts, 1)
            nc.gpsimd.memset(mask[:, :], 0.0).then_inc(consts, 1)
            nc.gpsimd.memset(neg_half[:, :], -0.5).then_inc(consts, 1)
            nc.gpsimd.iota(ranks[:, :], [[1, TOPK]], base=0, channel_multiplier=0,
                           allow_small_or_imprecise_dtypes=True).then_inc(consts, 1)
            pool.wait_ge(consts, 5)
            nc.gpsimd.affine_select(out=ident[:, :], in_=ident[:, :], pattern=[[-1, P]], compare_op=ALU.not_equal,
                                    fill=1.0, base=0, channel_multiplier=1).then_inc(consts, 1)
            nc.gpsimd.affine_select(out=upper[:, :], in_=ones[:, :], pattern=[[1, P]], compare_op=ALU.is_ge,
                                    fill=0.0, base=0, channel_multiplier=-1).then_inc(consts, 1)
            nc.gpsimd.affine_select(out=later[:, :], in_=ones[:, :], pattern=[[-1, P]], compare_op=ALU.is_gt,
                                    fill=0.0, base=0, channel_multiplier=1).then_inc(consts, 1)
            nc.gpsimd.affine_select(out=mask[:, P:], in_=mask[:, P:], pattern=[[-1, P]], compare_op=ALU.is_ge,
                                    fill=NEG, base=0, channel_multiplier=1).then_inc(consts, 1)

            def inverse_root(dst, src, n, done):
                step(nc.gpsimd.tensor_scalar(dst, src, 1.0 / n, EPS, ALU.mult, ALU.add))
                step.wait()
                nc.gpsimd.tensor_tensor(dst, dst, neg_half[0:dst.shape[0], :].to_broadcast(list(dst.shape)), ALU.pow)\
                    .then_inc(done, 1)

            def norm(n):
                tiles, _, _ = pieces(n)
                t0 = sum(NORM_TILES[:n])
                for k, (_, r, _) in enumerate(tiles):
                    pool.wait_ge(norm_ss, t0 + k + 1)
                    inverse_root(stat[0:r, 8 + k:9 + k], stat[0:r, k:k + 1], D, norm_rstd)

            def post(p):
                for j in range(TT):
                    pool.wait_ge(post_ss, 2 * p + j + 1)
                    inverse_root(stat[:, 12 + j:13 + j], stat[:, 4 + j:5 + j], D, post_rstd)

            norm(0)
            norm(1)
            pool.wait_ge(consts, 9)
            pool.wait_ge(logf, 1)
            zf = SQ[:, 0, 0:16].rearrange("p (j h) -> p j h", j=TT)
            for n, (j, m) in enumerate(((0, later), (1, ones), (1, later))):
                nc.gpsimd.tensor_tensor(DEC[:, :, n, :], zf[:, j, :][:, :, None].to_broadcast([P, FOX_H, P]),
                                        m[:, None, :].to_broadcast([P, FOX_H, P]), ALU.mult).then_inc(dec_done, 1)
            for p in range(3):
                post(p)
                norm(2 + p)
            pool.wait_ge(a_free, A_BASE["sc"] + 12)
            step(nc.gpsimd.memset(SP[:, :, 0:2], 0.0))
            step(nc.gpsimd.tensor_tensor(SP[:, :, 2:], SCX[:, SC_T:2 * SC_T, :], SCX[:, 2 * SC_T:, :], ALU.mult))
            step.wait()
            for k in range(SC_T):
                t0, t1 = sct[:, k % 2, :], SP_tmp[:, :]

                def tap(w):
                    return SP[:, k, META + w:META + w + T], colp[:, COL["sc_w"] + 3 * k + w:COL["sc_w"] + 3 * k + w + 1]

                if k >= 2:
                    pool.wait_ge(sc_lo, k - 1)
                a, wt = tap(0)
                step(nc.gpsimd.tensor_scalar(t0, a, wt, None, ALU.mult))
                for w in (1, 2):
                    a, wt = tap(w)
                    step(nc.gpsimd.tensor_scalar(t1, a, wt, None, ALU.mult))
                    step.wait()
                    step(nc.gpsimd.tensor_tensor(t0, t0, t1, ALU.add))
                    step.wait()
                nc.gpsimd.tensor_tensor(t0, t0, SCX[:, k, META:], ALU.mult).then_inc(sc_y, 1)
            pool.wait_ge(sc_lo, SC_T)

            def bc(t, r, w=SSD_D):
                return t[:, :, None].to_broadcast([r, SSD_H, w])

            def spread_xdd(c):
                r = META if c == 0 else P
                o = 96 if c == 0 else 48
                nc.gpsimd.tensor_tensor(XDD[0:r, :].rearrange("p (h d) -> p h d", h=SSD_H),
                                        XT[0:r, c, :].rearrange("p (h d) -> p h d", h=SSD_H),
                                        bc(exs[0:r, o:o + 24], r), ALU.mult).then_inc(xdd_done, 1)

            pool.wait_ge(tr_out, 3)
            pool.wait_ge(xdd_w, 2)
            spread_xdd(0)
            pool.wait_ge(tr_out, 11)

            def decay_inputs(k):
                c, s = divmod(k, 8)
                if k >= 2:
                    pool.wait_ge(seg_prod, k - 1)
                a = dtz[:, 3, 24 * (c + 1) + 3 * s:24 * (c + 1) + 3 * s + 3]
                nc.gpsimd.tensor_tensor(AU[:, k % 2, :, :], a[:, :, None].to_broadcast([P, 3, P]),
                                        upper[:, None, :].to_broadcast([P, 3, P]), ALU.mult).then_inc(au_done, 1)

            def spread_xdt(c):
                nc.gpsimd.tensor_tensor(XDT[:, c, :].rearrange("p (h d) -> p h d", h=SSD_H),
                                        XT[:, c + 1, :].rearrange("p (h d) -> p h d", h=SSD_H),
                                        bc(dtz[:, 2, 24 * (c + 1):24 * (c + 2)], P), ALU.mult).then_inc(xdt_done, 1)

            def skip(c):
                nc.gpsimd.tensor_tensor(XT[:, c + 1, :].rearrange("p (h d) -> p h d", h=SSD_H),
                                        XT[:, c + 1, :].rearrange("p (h d) -> p h d", h=SSD_H),
                                        bc(rowp[:, ROW["d_skip"]:ROW["d_skip"] + SSD_H], P), ALU.mult)\
                    .then_inc(xd_done, 1)

            def group_norm(c):
                pool.wait_ge(grp_ss, 4 * c + 4)
                inverse_root(stat[:, 28:32], stat[:, 24:28], GW, grp_rstd)

            decay_inputs(0)
            decay_inputs(1)
            spread_xdt(0)
            for k in range(2, 4):
                decay_inputs(k)
            pool.wait_ge(st_prod, SSD_G)
            spread_xdd(1)
            pool.wait_ge(xdt_done, 1)
            pool.wait_ge(xdd_done, 2)
            for k in range(4, 8):
                decay_inputs(k)
            skip(0)
            spread_xdt(1)
            pool.wait_ge(xdt_done, 2)
            for k in range(8, 12):
                decay_inputs(k)
            group_norm(0)
            skip(1)
            for k in range(12, 16):
                decay_inputs(k)
            group_norm(1)
            pool.wait_ge(w_used, LAST["wout2"])
            pool.dma_start(keys[:, :, :], keys_in).then_inc(keys_land, 16)
            pool.wait_ge(x_ready, 8)
            pool.dma_start(h2_spill, X[:, :, :]).then_inc(spilled, 16)
            norm(5)
            pool.wait_ge(spilled, 16)
            pool.wait_ge(norm_scaled, sum(NORM_TILES))
            nc.gpsimd.iota(numbers[:, :, :], [[1, KEYS], [0, BATCH]], base=0, channel_multiplier=0,
                           allow_small_or_imprecise_dtypes=True).then_inc(numbered, 1)
            for j in range(TT):
                pool.wait_ge(fin_ss, j + 1)
                inverse_root(stat[:, 12 + j:13 + j], stat[:, 4 + j:5 + j], D, fin_rstd)

        @block.tensor
        def _(pe):
            def mm(o, a, b, start, stop):
                return nc.tensor.matmul(o, a, b, start=start, stop=stop)

            def wide(name, j, rh, rl, n, i=0):
                b = STREAM[name] + j
                e = A_BASE[name] + j
                s = b % SLOTS
                pe.wait_ge(split_lo, i * 4 + (b + 1))
                if not (type(i) is int and 4 * i + e < 2):
                    pe.wait_ge(a_free, i * 4 + (e - 1))
                wide_products(s, e % 2, rh, rl, n).then_inc(w_used, 1)

            def wide_products(s, bank, rh, rl, n):
                for kt in range(KT):
                    h, l = wh[:, s, P * kt:P * kt + P], wl[:, s, P * kt:P * kt + P]
                    mm(AO[:, bank, 0:n], h, rh[:, kt, 0:n], kt == 0, False)
                    mm(AO[:, bank, 0:n], h, rl[:, kt, 0:n], False, False)
                    ins = mm(AO[:, bank, 0:n], l, rh[:, kt, 0:n], False, kt == KT - 1)
                return ins

            def flat(s, outs, ah, al, offs, first, last):
                for j in range(TT):
                    for n, o in enumerate(offs):
                        mm(outs[j][n], ah[j], wh[:, s, o:o + 512], first, False)
                        mm(outs[j][n], ah[j], wl[:, s, o:o + 512], False, False)
                        ins = mm(outs[j][n], al[j], wh[:, s, o:o + 512], False, last)
                return ins

            Y4 = [[Y[:, j, 0:512], Y[:, j, 512:1024]] for j in range(TT)]

            def flat_stage(name, n, ah, al):
                for kt in range(n):
                    b = STREAM[name] + kt
                    pe.wait_ge(split_lo, b + 1)
                    flat(b % SLOTS, Y4, [ah[:, kt, P * j:P * j + P] for j in range(TT)],
                         [al[:, kt, P * j:P * j + P] for j in range(TT)], (0, 512), kt == 0, kt == n - 1)\
                        .then_inc(w_used, 1)

            def half_stage(b0, half, ah, al, c0, between=None):
                for k in range(4):
                    pe.wait_ge(split_lo, b0 + k + 1)
                    for q in range(2):
                        kt = 2 * k + q
                        ins = flat((b0 + k) % SLOTS, [[Y4[half][j]] for j in range(TT)],
                                   [ah[:, kt, c0 + P * j:c0 + P * j + P] for j in range(TT)],
                                   [al[:, kt, c0 + P * j:c0 + P * j + P] for j in range(TT)],
                                   (512 * q,), kt == 0, kt == KT - 1)
                    ins.then_inc(w_used, 1)
                    if between:
                        between(k)

            def norm_part(n, k, q):
                _, r, _ = pieces(n)[0][k]
                t = sum(NORM_TILES[:n]) + k
                pe.wait_ge(norm_scaled, t + 1)
                g = 2 * t + q
                if g >= 2:
                    pe.wait_ge(norm_lo, g - 1)
                for i in range(4):
                    kt = 4 * q + i
                    ins = nc.tensor.transpose(M[:, g % 2, P * i:P * i + r], xn[0:r, k, P * kt:P * kt + P],
                                              ident[0:r, 0:r])
                ins.then_inc(norm_turned, 1)

            def norm(n):
                for k in range(NORM_TILES[n]):
                    for q in range(2):
                        norm_part(n, k, q)
                pe.wait_ge(norm_lo, 2 * sum(NORM_TILES[:n + 1]))

            def thin(outs, at, width):
                for o, r, c in outs:
                    for kt in range(KT):
                        e = slice(at + width * kt, at + width * kt + width)
                        for n, (part, w) in enumerate(((xh, thin_h), (xh, thin_l), (xl, thin_h))):
                            ins = mm(o, part[:, kt, c:c + r], w[:, e], kt == 0 and n == 0, kt == KT - 1 and n == 2)
                return ins

            pe.wait_ge(consts, 9)
            norm(0)
            for j in range(8):
                wide("ag", j, xh, xl, T)
            for j in range(8):
                wide("qk", j, xh, xl, T)
                if 2 <= j < 6:
                    norm_part(1, (j - 2) // 2, j % 2)
            half_stage(STREAM["v"], 0, xh, xl, 0)
            pe.wait_ge(thin_lo, 1)
            pe.wait_ge(norm_lo, 2 * (NORM_TILES[0] + NORM_TILES[1]))
            thin([(M[:, 0, 8 * j:8 * j + 8], P, P * j) for j in range(TT)],
                 0, FOX_H).then_inc(f_prod, 1)
            for j in range(4):
                wide("mk", j, mh, ml, T)
            half_stage(STREAM["mv"], 1, mh, ml, 0)
            pe.wait_ge(logf, 1)
            pe.wait_ge(a_free, A_BASE["mk"] + 4)

            def layer_norm(s):
                if s == LN_AT[0]:
                    pe.wait_ge(conv_done, 1)
                    for c in range(CT):
                        ins = mm(AO[:, 0, 0:T], ones[:, :], CV[:, c, :], c == 0, c == CT - 1)
                    ins.then_inc(ln_sum, 1)
                if s == LN_AT[1]:
                    pe.wait_ge(ln_sq, 1)
                    for c in range(CT):
                        ins = mm(AO[:, 1, 0:T], ones[:, :], SQ[:, c, :], c == 0, c == CT - 1)
                    ins.then_inc(ln_sum, 1)

            pe.wait_ge(dec_done, 3)
            pe.wait_ge(v_out, 1)
            pe.wait_ge(mv_out, 1)

            def attention(first, last, between=None):
                for s in range(first, last + 3):
                    if between:
                        between(s)
                    u = s
                    if u < last:
                        kind, h, j = units[u]
                        o = M[:, u % 2, :]
                        if u >= 2:
                            pe.wait_ge(at_max, u - 1)
                        if kind == "fox":
                            r = slice(FOX_D * (h % 2), FOX_D * (h % 2) + FOX_D)
                            q, k = QK[r, h // 2, P * j:P * j + P], QK[r, CT + h // 2, 0:P * (j + 1)]
                            mm(o[:, 0:P * (j + 1)], q, k, True, False)
                            if j == 0:
                                ins = mm(o[:, 0:P], upper[:, :], DEC[:, h, 0, :], False, True)
                            else:
                                mm(o[:, 0:P], ones[:, :], DEC[:, h, 0, :], False, False)
                                ins = mm(o[:, 0:2 * P], upper[:, :],
                                         DEC[:, h, 1:3, :].rearrange("p a b -> p (a b)"), False, True)
                        else:
                            ins = mm(o[:, 0:T], MQ[:, h, P * j:P * j + P], MK[:, h, :], True, True)
                        ins.then_inc(at_logit, 1)
                    u = s - 2
                    if first <= u < last:
                        pe.wait_ge(at_p, u + 1)
                        if u >= 2:
                            pe.wait_ge(at_pt, u - 1)
                        for kt in range(unit_keys(u) // P):
                            ins = nc.tensor.transpose(Y[:, 0, 512 * (u % 2) + P * kt:512 * (u % 2) + P * kt + P],
                                                      att_p[:, u % 2, P * kt:P * kt + P], ident[:, :])
                        ins.then_inc(at_turn, 1)
                    u = s - 3
                    if first <= u < last:
                        kind, h, j = units[u]
                        pe.wait_ge(at_pt, u + 1)
                        if u >= 2:
                            pe.wait_ge(at_lo, u - 1)
                        n = unit_keys(u) // P
                        vals, v = (V, h // 2) if kind == "fox" else (MV, h)
                        for kt in range(n):
                            ins = mm(Y[:, 1, 512 * (u % 2):512 * (u % 2) + P], vals[:, kt, P * v:P * v + P],
                                     att_pt[:, u % 2, kt, :], kt == 0, kt == n - 1)
                        ins.then_inc(at_pv, 1)

            attention(0, fox_units, layer_norm)
            pe.wait_ge(at_lo, fox_units)
            pe.wait_ge(ln_lo, 1)
            flat_stage("wout", 8, mixh, mixl)
            norm(2)
            for j in range(4):
                wide("mq", j, xh, xl, T)
            pe.wait_ge(a_free, A_BASE["mq"] + 4)
            attention(fox_units, len(units))
            pe.wait_ge(at_lo, len(units))
            flat_stage("mo", 4, moh, mol)
            norm(3)

            def mlp(name, n, ah, al, base):
                b0 = STREAM[name]

                def up(s, i, bank):
                    b = b0 + 2 * s - 1
                    pe.wait_ge(split_lo, i * 4 + (b + 1))
                    pe.wait_ge(a_free, i * 2 + (A_BASE[name] + s - 1))
                    wide_products(b % SLOTS, bank, xh, xl, T).then_inc(w_used, 1)

                def down(b, s, i, first, last):
                    pe.wait_ge(split_lo, i * 4 + (b + 1))
                    pe.wait_ge(hid_lo, i * 2 + (base + s + 1))
                    flat(b % SLOTS, Y4, [ah[:, s, P * j:P * j + P] for j in range(TT)],
                         [al[:, s, P * j:P * j + P] for j in range(TT)], (0, 512), first, last).then_inc(w_used, 1)

                pe.wait_ge(split_lo, b0 + 1)
                wide_products(b0 % SLOTS, A_BASE[name] % 2, xh, xl, T).then_inc(w_used, 1)
                for s in range(2):
                    up(s + 1, 0, (s + 1) % 2)
                    down(b0 + 2 + 2 * s, s, 0, s == 0, False)
                with pe.Fori(1, n // 2 - 1) as i:
                    for s in range(2):
                        up(s + 1, i, (s + 1) % 2)
                        down(b0 + 2 + 2 * s, s, i, False, False)
                i = n // 2 - 1
                up(1, i, 1)
                down(b0 + 2, 0, i, False, False)
                down(down_block(b0, n - 1, n) - 4 * i, 1, i, False, True)

            mlp("mlp", FF_CHUNKS, mlp_ah, mlp_al, 0)
            norm(4)
            thin([(M[0:META, 0, 0:24], META, 0)] + [(M[:, 0, 24 * (j + 1):24 * (j + 2)], P, META + P * j)
                                                    for j in range(TT)],
                 KT * FOX_H, SSD_H).then_inc(dt_prod, 1)
            with pe.Fori(0, XBC_T // 4) as i:
                for j in range(4):
                    wide("xbc", j, xh, xl, TM, i)
            with pe.Fori(0, SC_T * 3 // 4) as i:
                for j in range(4):
                    wide("sc", j, xh, xl, TM, i)
            pe.wait_ge(x_ready, 6)
            pe.wait_ge(xsilu, XBC_T // 4)
            pe.wait_ge(dt_a, 2)
            turned = turned_tiles()

            def turn(n):
                if n >= len(turned):
                    return
                _, r, t0, q = turned[n]
                if n >= 2:
                    pe.wait_ge(tr_out, n - 1)
                for i in range(4):
                    ins = nc.tensor.transpose(M[0:r, n % 2, P * i:P * i + P], XS[:, 4 * q + i, t0:t0 + r],
                                              ident[:, :])
                ins.then_inc(tr_in, 1)

            for g in range(3):
                if g == 2:
                    pe.wait_ge(z_out, 1)
                half_stage(STREAM["z"] + 4 * g, g % 2, xh, xl, META, lambda k: turn(4 * g + k))
            pe.wait_ge(a_free, A_BASE["sc"] + 12)
            a1, a2, a0 = dtz[:, 3, 24:48], dtz[:, 3, 48:72], dtz[0:META, 3, 0:24]
            mm(AO[:, 1, 0:24], upper[:, :], a1, True, True)
            mm(AO[:, 1, 24:48], upper[:, :], a2, True, True)
            mm(AO[:, 1, 48:72], later[:, :], a1, True, True)
            mm(AO[:, 1, 72:96], ones[:, :], a1, True, True)
            mm(AO[0:META, 1, 96:120], later[0:META, 0:META], a0, True, True).then_inc(ac_prod, 1)
            pe.wait_ge(tr_out, 11)
            pe.wait_ge(xdd_done, 1)
            for g in range(SSD_G):
                if g >= 2:
                    pe.wait_ge(st_done, g - 1)
                mm(M[:, g % 2, 0:GW], BN[0:META, 0, P * g:P * g + P], XDD[0:META, GW * g:GW * g + GW], True, True)\
                    .then_inc(st_prod, 1)
            pe.wait_ge(st_done, SSD_G)
            pe.wait_ge(z_out, 3)
            for c in range(TT):
                tok = slice(META + P * c, META + P * c + P)
                if c:
                    pe.wait_ge(st_done, 2 * SSD_G)
                    pe.wait_ge(y_add, 1)
                for g in range(SSD_G):
                    ins = mm(M[:, 0, P * g:P * g + P], XS[:, XS_T + g, tok], XS[:, XS_T + SSD_G + g, tok], True, True)
                ins.then_inc(cb_prod, 1)
                pe.wait_ge(xdt_done, c + 1)

                def seg(s):
                    k = 8 * c + s
                    pe.wait_ge(au_done, k + 1)
                    if k < 2:
                        pe.wait_ge(ac_exp, 2)
                    else:
                        pe.wait_ge(seg_exp, k - 1)
                    mm(AO[:, k % 2, 0:3 * P], later[:, :], AU[:, k % 2, :, :].rearrange("p a b -> p (a b)"),
                       True, True).then_inc(seg_prod, 1)

                seg(0)
                for s in range(8):
                    if s < 7:
                        seg(s + 1)
                    if s % 2 == 0:
                        g = s // 2
                        if g == 0:
                            pe.wait_ge(cb_mask, c + 1)
                        else:
                            pe.wait_ge(off_done, 4 * c + g - 1) if 4 * c + g - 1 > 0 else None
                        mm(M[:, (g + 1) % 2, 0:GW], XS[:, XS_T + SSD_G + g, tok], ST[:, GW * g:GW * g + GW],
                           True, True).then_inc(off_prod, 1)
                    k = 8 * c + s
                    pe.wait_ge(seg_m, k + 1)
                    yd = Y[:, :, :].rearrange("p a b -> p (a b)")
                    for t in range(3):
                        h = 3 * s + t
                        ins = mm(yd[:, SSD_D * h:SSD_D * h + SSD_D], MM[:, k % 2, t, :],
                                 XDT[:, c, SSD_D * h:SSD_D * h + SSD_D], True, True)
                    ins.then_inc(y_prod, 1)
                if c == 0:
                    pe.wait_ge(xdd_done, 2)
                    pe.wait_ge(off_done, 4)
                    for g in range(SSD_G):
                        if g >= 2:
                            pe.wait_ge(st_done, SSD_G + g - 1)
                        mm(M[:, g % 2, 0:GW], BN[:, 1, P * g:P * g + P], XDD[:, GW * g:GW * g + GW], True, True)\
                            .then_inc(st_prod, 1)
            pe.wait_ge(sc_lo, SC_T)
            pe.wait_ge(y_add, 4)
            pe.wait_ge(off_done, 8)

            def turn_y(k):
                c, q = divmod(k, 3)
                pe.wait_ge(grp_y, 4 * c + 4)
                if k >= 2:
                    pe.wait_ge(y_lo, k - 1)
                for i in range(4):
                    ins = nc.tensor.transpose(M[:, k % 2, P * i:P * i + P],
                                              YO[c][:, P * (4 * q + i):P * (4 * q + i) + P], ident[:, :])
                ins.then_inc(y_turn, 1)

            for j in range(16):
                kt = (j - SC_T) % 16
                if j >= SC_T:
                    pe.wait_ge(y_lo, min(4 + (j - SC_T) // 4, 6))
                b = STREAM["wout2"] + j
                pe.wait_ge(split_lo, b + 1)
                flat(b % SLOTS, Y4, [m2h[:, kt, P * c:P * c + P] for c in range(TT)],
                     [m2l[:, kt, P * c:P * c + P] for c in range(TT)], (0, 512), j == 0, j == 15).then_inc(w_used, 1)
                for k in range(6):
                    if TURN_AT[k] == j:
                        turn_y(k)
            norm(5)
            with pe.Fori(0, 4) as i:
                for j in range(4):
                    wide("wq", j, xh, xl, T, i)
            pe.wait_ge(a_free, A_BASE["wq"] + 16)
            pe.wait_ge(keys_land, 16)
            for q in range(8):
                j = q // 4
                if q >= 4:
                    pe.wait_ge(s_out, q - 3)
                for n in range(4):
                    hs = 4 * (q % 4) + n
                    ins = mm(Y[:, (q // 2) % 2, 512 * (q % 2) + P * n:512 * (q % 2) + P * n + P],
                             QP[:, hs, P * j:P * j + P], keys[:, hs, :], True, True)
                ins.then_inc(s_prod, 1)
            def up(s, b, bank, e, i=0):
                pe.wait_ge(split_lo, i * 4 + (b + 1))
                wide_products(b % SLOTS, bank, xh, xl, T).then_inc(w_used, 1)

            with pe.Fori(0, HALF // 4) as i:
                for s in range(4):
                    pe.wait_ge(a_free, i * 4 + (A_BASE["peer"] + s - 1))
                    up(s, P0 + s, s % 2, 0, i)
            for j in range(TT):
                pe.wait_ge(top_nat, j + 1)
                for n in range(3):
                    ins = nc.tensor.transpose(M[:, j, P * n:P * n + P], NAT[:, j, n, :], ident[:, :])
                ins.then_inc(top_turn, 1)

            def spread(base, c, bank, A, B):
                pe.wait_ge(hot_b, c * 5 + 5 * (base + 1))
                for t in range(BATCH):
                    for n in range(3):
                        ins = mm(M[:, bank, WIN * t:WIN * t + WIN], A[:, :, t], B[:, n, :, t], n == 0, n == 2)
                ins.then_inc(g_prod, 1)

            pe.wait_ge(s_out, 8)
            sets = ((hotA, hotB), (hotA2, hotB2))
            for s in range(2):
                spread(0, s, s, *sets[s])
            with pe.Fori(1, WIN // 2) as i:
                for s in range(2):
                    pe.wait_ge(g_out, i * 2 + (s - 1))
                    spread(0, i * 2 + s, s, *sets[s])

            def down(n, b, s, i, first, last):
                pe.wait_ge(split_lo, i * 4 + (b + 1))
                pe.wait_ge(hid_lo, n + (FF_CHUNKS + 1))
                flat(b % SLOTS, Y4, [peer_ah[:, s, P * j:P * j + P] for j in range(TT)],
                     [peer_al[:, s, P * j:P * j + P] for j in range(TT)], (0, 512), first, last).then_inc(w_used, 1)

            def next_gates(w, c, s):
                pe.wait_ge(g_out, c + (WIN * w - 1))
                spread(WIN * w, c, s, hotA, hotB)

            def both(c, s, i, w, first):
                pe.wait_ge(a_free, c + (A_BASE["peer"] + HALF - 1))
                up(s, P0 + HALF + 2 * s, s, 0, i)
                next_gates(w + 1, c + (-WIN * w), s)
                down(c, P0 + HALF + 1 + 2 * s, s, i, first, False)

            for w in range(2):
                if w == 0:
                    both(0, 0, 0, 0, True)
                    both(1, 1, 0, 0, False)
                with pe.Fori(WIN // 2 * w + (w == 0), WIN // 2 * (w + 1)) as i:
                    for s in range(2):
                        both(i * 2 + s, s, i, w, False)
            for w in range(2, 4):
                with pe.Fori(8 * w - 16, 8 * w - 8 - (w == 3)) as i:
                    for s in range(4):
                        if w == 2:
                            next_gates(3, i * 4 + s, s % 2)
                        down(i * 4 + (HALF + s), P0 + 3 * HALF + s, s % 2, i, False, False)
            for s in range(4):
                down(KEYS - 4 + s, P0 + 3 * HALF + s, s % 2, HALF // 4 - 1, False, s == 3)


def kernel(**inputs):
    import concourse.bacc as _bacc
    from concourse.bass_utils import run_bass_kernel_spmd as _run

    a = {k: np.asarray(v) for k, v in inputs.items()}

    def wide_blocks(w):
        return w.reshape(KT, P, -1, P).transpose(2, 1, 0, 3).reshape(-1, P, BLK)

    def flat_blocks(w):
        return w.reshape(-1, P, BLK)

    def half_blocks(w):
        return w.reshape(4, 2, P, 512).transpose(0, 2, 1, 3).reshape(-1, P, BLK)

    def mlp_blocks(up, down):
        u, d = wide_blocks(up), flat_blocks(down)
        n = len(u)
        order = [u[0:1]]
        for c in range(n - 1):
            order += [u[c + 1:c + 2], d[c:c + 1]]
        return np.concatenate(order + [d[n - 1:n]])

    def peer_blocks(up, down):
        u, d = wide_blocks(up), flat_blocks(down)
        pairs = np.stack([u[HALF:], d[:HALF]], 1).reshape(-1, P, BLK)
        return np.concatenate([u[:HALF], pairs, d[HALF:]])

    w_in, w2 = a["w_in"][0], a["w_in_2"][0]
    c1, c2, c3, c4 = CONV_CH * 2, CONV_CH * 2 + 1024, CONV_CH * 2 + 1536, w_in.shape[1]
    z1, z2, z3 = D_SSD, D_SSD + XBC_T * P, D_SSD + XBC_T * P + SSD_H
    stream = np.concatenate([
        wide_blocks(w_in[:, 0:c1]), wide_blocks(w_in[:, c1:c2]), half_blocks(w_in[:, c2:c3]),
        wide_blocks(a["w_mk"][0]), half_blocks(a["w_mv"][0]), flat_blocks(a["w_out"][0]),
        wide_blocks(a["w_mq"][0]), flat_blocks(a["w_mo"][0]), mlp_blocks(a["w_up"][0], a["w_down"][0]),
        wide_blocks(w2[:, z1:z2]), wide_blocks(w2[:, z3:]),
        *[half_blocks(w2[:, 512 * g:512 * g + 512]) for g in range(3)], np.roll(flat_blocks(a["w_out_2"][0]), SC_T, 0),
        wide_blocks(a["w_q_2"][0]), peer_blocks(a["expert_u_2"][0].T, a["expert_v_2"][0])])
    assert stream.shape == (N_BLOCKS, P, BLK)

    def on_partitions(v, n):
        v = v.reshape(-1, n, P)
        return v.transpose(2, 1, 0).reshape(P, -1)

    gain_cols = np.concatenate([on_partitions(a[k], KT) for k in (
        "norm_mix_pre", "norm_memkv", "norm_mem_pre", "norm_mlp_pre", "g_mix_2", "g_ffn_2")], 1)
    cols = np.concatenate([
        on_partitions(a["conv_w"][0], CT), on_partitions(a["conv_b"], CT), on_partitions(a["conv_ln_g"], CT),
        on_partitions(a["conv_ln_b"], CT), on_partitions(a["conv_ssd_w_2"][0], XBC_T),
        on_partitions(a["conv_ssd_b_2"], XBC_T), on_partitions(a["conv_sc_w_2"][0], SC_T),
        w_in[:, c3:c4].reshape(KT, P, FOX_H).transpose(1, 0, 2).reshape(P, -1),
        w2[:, z2:z3].reshape(KT, P, SSD_H).transpose(1, 0, 2).reshape(P, -1)], 1)
    rows = np.concatenate([a[k].reshape(-1) for k in ("b_forget", "dt_bias_2", "a_log_2", "d_skip_2", "ssd_norm_w_2")])
    post = np.stack([a[k].reshape(-1) for k in ("norm_mix_post", "norm_mem_post", "norm_mlp_post", "g_final_2")])
    keys_in = a["sub_keys_2"][0].reshape(16, KEYS, P).transpose(2, 0, 1)
    arrays = {
        "in_stream": stream, "in_gains": gain_cols, "in_cols": cols, "in_rows": rows, "in_post": post,
        "in_x": a["x"][0].reshape(TT, P, D).transpose(1, 0, 2), "in_mem": a["mem"][0].reshape(TT, P, D).transpose(1, 0, 2),
        "in_meta": a["meta_tokens_2"], "in_keys": keys_in,
    }
    arrays = {k: np.ascontiguousarray(v) for k, v in arrays.items()}
    nc = _bacc.Bacc("TRN2", target_bir_lowering=False, num_devices=1)
    ap = {k: nc.dram_tensor(k, v.shape, F32, kind="ExternalInput").ap() for k, v in arrays.items()}
    out = nc.dram_tensor("out_x", (P, TT, D), F32, kind="ExternalOutput").ap()
    spill = nc.dram_tensor("h2_spill", (P, TT, D), F32).ap()
    build(nc, ap["in_stream"], ap["in_gains"], ap["in_cols"], ap["in_rows"], ap["in_post"], ap["in_x"],
          ap["in_mem"], ap["in_meta"], ap["in_keys"], out, spill)
    r = _run(nc, [arrays], core_ids=[0])
    got = r.results[0]["out_x"]
    return np.ascontiguousarray(got.transpose(1, 0, 2).reshape(1, T, D))
```
